# Optimizing a Trainium2 kernel written in Bass

```python
import math
import jax, jax.numpy as jnp
from jax import lax
import numpy as np

D_MODEL = 1024
BATCH = 1
SEQ = 128
DEPTH = 1
DEC_BATCH = 1
DEC_SEQ = 512
PAST_LEN = 128

GRID_W = 64
D_SSM = D_MODEL // 2
SSM_CH = 16
N_SSM_GROUPS = D_SSM // SSM_CH
SSM_STATE = 64
D_CONV = D_MODEL // 2
CONV_HEADS = 8
CONV_WIDTH = 3
D_MIX = D_SSM + D_CONV
D_IN = D_SSM + 3 * D_CONV
N_MOD = 6
PEER_HEADS = 8
PEER_NKEYS = 128
PEER_TOPK = 16
PEER_DQ = D_MODEL // 4
N_EXPERTS = PEER_NKEYS ** 2
TOKEN_BLOCK = 128
EPS = 1e-6

kernel_name = "hybrid_s5_shortconv_peer_diffusion_step"

def rmsnorm(x, g):
    xf = x.astype(jnp.float32)
    y = xf * lax.rsqrt(jnp.mean(xf * xf, axis=-1, keepdims=True) + EPS)
    return (y * g.astype(jnp.float32)).astype(x.dtype)

def _combine(left, right):
    a1, b1 = left
    a2, b2 = right
    return a1 * a2, a2 * b1 + b2

def s5_scan(u, h0, lam_re, lam_im, log_dt, b_re, b_im, c_re, c_im, reverse):
    f32 = jnp.float32
    lam = lax.complex(lam_re.astype(f32), lam_im.astype(f32))
    dt = jnp.exp(log_dt.astype(f32))[:, None]
    a_bar = jnp.exp(lam * dt)
    b_mat = lax.complex(b_re.astype(f32), b_im.astype(f32))
    b_bar = ((a_bar - 1.0) / lam)[..., None] * b_mat
    c_mat = lax.complex(c_re.astype(f32), c_im.astype(f32))
    bu = jnp.einsum("gnp,blgp->blgn", b_bar, u.astype(f32).astype(jnp.complex64))
    a = jnp.broadcast_to(a_bar, bu.shape)
    a_cum, h = lax.associative_scan(_combine, (a, bu), reverse=reverse, axis=1)
    h = h + a_cum * h0[:, None]
    y = jnp.einsum("gpn,blgn->blgp", c_mat, h).real
    h_last = h[:, 0] if reverse else h[:, -1]
    return y, h_last

def ssm_mixer(u, h0_f, h0_b, p):
    bn, seq_len, _ = u.shape
    ug = u.reshape(bn, seq_len, N_SSM_GROUPS, SSM_CH)
    y_f, h_f = s5_scan(ug, h0_f, p["lam_re"][0], p["lam_im"][0], p["log_dt"][0], p["b_re"][0], p["b_im"][0],
                       p["c_re"][0], p["c_im"][0], reverse=False)
    y_b, h_b = s5_scan(ug, h0_b, p["lam_re"][1], p["lam_im"][1], p["log_dt"][1], p["b_re"][1], p["b_im"][1],
                       p["c_re"][1], p["c_im"][1], reverse=True)
    y = (y_f + y_b).reshape(bn, seq_len, D_SSM) + p["d_skip"].astype(jnp.float32) * u.astype(jnp.float32)
    g = jax.nn.gelu(y)
    out = g * jax.nn.sigmoid(g @ p["w_glu"].astype(jnp.float32) + p["b_glu"].astype(jnp.float32))
    return out.astype(u.dtype), h_f, h_b

def short_conv(v, w, b, rows):
    bn, seq_len, ch = v.shape
    width = seq_len // rows
    vg = v.reshape(bn, rows, width, ch)
    vp = jnp.pad(vg, ((0, 0), (0, 0), (CONV_WIDTH // 2, CONV_WIDTH // 2), (0, 0)))
    y = sum(w[k] * vp[:, :, k:k + width] for k in range(CONV_WIDTH)) + b
    return y.reshape(bn, seq_len, ch)

def token_mixer(h, h0_f, h0_b, rows, p):
    bn, seq_len, _ = h.shape
    z = h @ p["w_in"]
    u, cb, cc, ch = jnp.split(z, [D_SSM, D_SSM + D_CONV, D_SSM + 2 * D_CONV], axis=-1)
    y_ssm, h_f, h_b = ssm_mixer(u, h0_f, h0_b, p)
    y_conv = cb * short_conv(cc * ch, p["conv_w"], p["conv_b"], rows)
    g = p["out_norm_g"]
    y_ssm = rmsnorm(y_ssm, g[:D_SSM])
    hd = D_CONV // CONV_HEADS
    y_conv = rmsnorm(y_conv.reshape(bn, seq_len, CONV_HEADS, hd), g[D_SSM:].reshape(CONV_HEADS, hd))
    y = jnp.concatenate([y_ssm, y_conv.reshape(bn, seq_len, D_CONV)], axis=-1)
    return y @ p["w_out"], h_f, h_b

def peer(h, w_query, sub_keys, expert_u, expert_v):
    bn, seq_len, d = h.shape
    xs = h.reshape(-1, TOKEN_BLOCK, d)
    sk = sub_keys.astype(jnp.float32)

    def block(xb):
        q = (xb @ w_query).astype(jnp.float32).reshape(TOKEN_BLOCK, PEER_HEADS, 2, PEER_DQ // 2)
        s = jnp.einsum("thse,sne->thsn", q, sk)
        s1, i1 = lax.top_k(s[:, :, 0], PEER_TOPK)
        s2, i2 = lax.top_k(s[:, :, 1], PEER_TOPK)
        cand = (s1[..., :, None] + s2[..., None, :]).reshape(TOKEN_BLOCK, PEER_HEADS, PEER_TOPK * PEER_TOPK)
        cidx = (i1[..., :, None] * PEER_NKEYS + i2[..., None, :]).reshape(TOKEN_BLOCK, PEER_HEADS, PEER_TOPK * PEER_TOPK)
        top, pos = lax.top_k(cand, PEER_TOPK)
        idx = jnp.take_along_axis(cidx, pos, axis=-1)
        gate = jax.nn.softmax(top, axis=-1)
        hid = jnp.einsum("thkd,td->thk", expert_u[idx], xb).astype(jnp.float32)
        act = (jax.nn.gelu(hid) * gate).astype(xb.dtype)
        return jnp.einsum("thk,thkd->td", act, expert_v[idx])

    return lax.map(block, xs).reshape(bn, seq_len, d)

def modulation(cond, w_mod, b_mod):
    m = jax.nn.silu(cond.astype(jnp.float32)) @ w_mod.astype(jnp.float32) + b_mod.astype(jnp.float32)
    return jnp.split(m, N_MOD, axis=-1)

def layer(x, cond, h0_f, h0_b, rows, p):
    sh1, sc1, g1, sh2, sc2, g2 = [m.astype(x.dtype) for m in modulation(cond, p["w_mod"], p["b_mod"])]
    h = rmsnorm(x, p["norm1_g"]) * (1 + sc1) + sh1
    y, h_f, h_b = token_mixer(h, h0_f, h0_b, rows, p)
    x = x + g1 * y
    h = rmsnorm(x, p["norm2_g"]) * (1 + sc2) + sh2
    x = x + g2 * peer(h, p["w_query"], p["sub_keys"], p["expert_u"], p["expert_v"])
    return x, h_f, h_b

def setup_inputs(seed: int = 0) -> dict:
    key = jax.random.key(seed)
    ks = jax.random.split(key, 32)
    f32 = jnp.float32

    def nrm(k, shape, scale):
        return scale * jax.random.normal(k, shape, f32)

    g_shape = (DEPTH, 2, N_SSM_GROUPS, SSM_STATE)
    n_idx = jnp.arange(SSM_STATE, dtype=f32)
    return {
        "x_prompt": nrm(ks[0], (BATCH, SEQ, D_MODEL), 1.0),
        "x_sample": nrm(ks[1], (DEC_BATCH, DEC_SEQ, D_MODEL), 1.0),
        "state_ssm_re": nrm(ks[2], (DEC_BATCH, DEPTH, 2, N_SSM_GROUPS, SSM_STATE), 0.1),
        "state_ssm_im": nrm(ks[3], (DEC_BATCH, DEPTH, 2, N_SSM_GROUPS, SSM_STATE), 0.1),
        "c": nrm(ks[4], (DEC_BATCH, D_MODEL), 1.0),
        "c_ctx": nrm(ks[5], (D_MODEL,), 1.0),
        "w_mod": nrm(ks[6], (DEPTH, D_MODEL, N_MOD * D_MODEL), 0.5 * D_MODEL ** -0.5),
        "b_mod": nrm(ks[7], (DEPTH, N_MOD * D_MODEL), 0.02),
        "norm1_g": 1.0 + nrm(ks[8], (DEPTH, D_MODEL), 0.05),
        "norm2_g": 1.0 + nrm(ks[9], (DEPTH, D_MODEL), 0.05),
        "w_in": nrm(ks[10], (DEPTH, D_MODEL, D_IN), D_MODEL ** -0.5),
        "lam_re": -0.5 + nrm(ks[11], g_shape, 0.01),
        "lam_im": math.pi * n_idx + nrm(ks[12], g_shape, 0.01),
        "log_dt": jax.random.uniform(ks[13], (DEPTH, 2, N_SSM_GROUPS), f32, math.log(1e-3), math.log(1e-1)),
        "b_re": nrm(ks[14], (DEPTH, 2, N_SSM_GROUPS, SSM_STATE, SSM_CH), (2 * SSM_CH) ** -0.5),
        "b_im": nrm(ks[15], (DEPTH, 2, N_SSM_GROUPS, SSM_STATE, SSM_CH), (2 * SSM_CH) ** -0.5),
        "c_re": nrm(ks[16], (DEPTH, 2, N_SSM_GROUPS, SSM_CH, SSM_STATE), (2 * SSM_STATE) ** -0.5),
        "c_im": nrm(ks[17], (DEPTH, 2, N_SSM_GROUPS, SSM_CH, SSM_STATE), (2 * SSM_STATE) ** -0.5),
        "d_skip": nrm(ks[18], (DEPTH, D_SSM), 1.0),
        "w_glu": nrm(ks[19], (DEPTH, D_SSM, D_SSM), D_SSM ** -0.5),
        "b_glu": nrm(ks[20], (DEPTH, D_SSM), 0.02),
        "conv_w": nrm(ks[21], (DEPTH, CONV_WIDTH, D_CONV), 0.5),
        "conv_b": nrm(ks[22], (DEPTH, D_CONV), 0.02),
        "out_norm_g": 1.0 + nrm(ks[23], (DEPTH, D_MIX), 0.05),
        "w_out": nrm(ks[24], (DEPTH, D_MIX, D_MODEL), D_MIX ** -0.5),
        "w_query": nrm(ks[25], (DEPTH, D_MODEL, PEER_HEADS * PEER_DQ), D_MODEL ** -0.5),
        "sub_keys": nrm(ks[26], (DEPTH, 2, PEER_NKEYS, PEER_DQ // 2), (PEER_DQ // 2) ** -0.5),
        "expert_u": nrm(ks[27], (DEPTH, N_EXPERTS, D_MODEL), D_MODEL ** -0.5),
        "expert_v": nrm(ks[28], (DEPTH, N_EXPERTS, D_MODEL), 0.5),
        "final_norm_g": 1.0 + nrm(ks[29], (D_MODEL,), 0.05),
    }

def reference(x_prompt, x_sample, state_ssm_re, state_ssm_im, c, c_ctx, w_mod, b_mod, norm1_g, norm2_g, w_in,
              lam_re, lam_im, log_dt, b_re, b_im, c_re, c_im, d_skip, w_glu, b_glu, conv_w, conv_b,
              out_norm_g, w_out, w_query, sub_keys, expert_u, expert_v, final_norm_g):
    f32 = jnp.float32
    rows = x_sample.shape[1] // GRID_W
    xp, xs = x_prompt, x_sample
    zero_state = jnp.zeros((x_prompt.shape[0], N_SSM_GROUPS, SSM_STATE), jnp.complex64)
    ctx_states = []
    for l in range(DEPTH):
        p = {
            "w_mod": w_mod[l], "b_mod": b_mod[l], "norm1_g": norm1_g[l], "norm2_g": norm2_g[l],
            "w_in": w_in[l], "lam_re": lam_re[l], "lam_im": lam_im[l], "log_dt": log_dt[l],
            "b_re": b_re[l], "b_im": b_im[l], "c_re": c_re[l], "c_im": c_im[l], "d_skip": d_skip[l],
            "w_glu": w_glu[l], "b_glu": b_glu[l], "conv_w": conv_w[l], "conv_b": conv_b[l],
            "out_norm_g": out_norm_g[l], "w_out": w_out[l], "w_query": w_query[l], "sub_keys": sub_keys[l],
            "expert_u": expert_u[l], "expert_v": expert_v[l],
        }
        xp, h_f, h_b = layer(xp, c_ctx[None, None, :], zero_state, zero_state, 1, p)
        ctx_states.append(jnp.stack([h_f, h_b], axis=1))
        h0_f = lax.complex(state_ssm_re[:, l, 0].astype(f32), state_ssm_im[:, l, 0].astype(f32))
        h0_b = lax.complex(state_ssm_re[:, l, 1].astype(f32), state_ssm_im[:, l, 1].astype(f32))
        xs, _, _ = layer(xs, c[:, None, :], h0_f, h0_b, rows, p)
    new_state = jnp.stack(ctx_states, axis=1)
    y_prompt = rmsnorm(xp, final_norm_g)
    y_sample = rmsnorm(xs, final_norm_g)
    return (y_prompt, y_sample, new_state.real, new_state.imag)


_drawn_inputs = setup_inputs


def setup_inputs(seed=0):
    import zlib

    import numpy as np

    out = dict(_drawn_inputs(seed))
    spreads = {}
    factors = {'state_ssm_re': 4.747,
     'state_ssm_im': 4.78,
     'norm2_g': 2.813,
     'lam_re': 4.541,
     'c_re': 2.743,
     'c_im': 2.801,
     'b_glu': 8.0,
     'conv_b': 7.373,
     'out_norm_g': 3.147}
    for name, (base, spread) in spreads.items():
        noise = np.random.default_rng([zlib.crc32(name.encode()), seed]).standard_normal(out[name].shape)
        drawn = base * np.exp(spread * noise) if base else spread * noise
        out[name] = __import__('jax').numpy.asarray(drawn.astype(out[name].dtype))
    for name, factor in factors.items():
        out[name] = (out[name] * factor).astype(out[name].dtype)
    return out
```

```python
from contextlib import ExitStack

import concourse.bass as bass
from concourse import mybir

F32 = mybir.dt.float32
U32 = mybir.dt.uint32
I32 = mybir.dt.int32
ALU = mybir.AluOpType
ACT = mybir.ActivationFunctionType
AX = mybir.AxisListType

P = 128
D = 1024
KD = D // P
CTX = 128
LAT = 512
T = CTX + LAT
NBLK = T // P
ROW_W = 64
DS = D // 2
DC = D // 2
KS = DS // P
GC = 16
NG = DS // GC
NPAIR = NG // 2
NS = 64
Q = 8
NCC = CTX // Q
NCL = LAT // Q
NCH = NCC + NCL
NQ = 2 * NPAIR
NLAG = 2 * Q - 1
NMOD = 6
NMT = NMOD * KD
MCH = 2
HEADS = 8
TOPK = 16
NKEY = 128
DQ = 256
SLOTS = 8
EPS = 1e-6
NEG = -3.0e38
TWO_PI = 6.283185307179586
PI_IN = 3.1415925
C1 = 6.28125
C2 = 0.0019350051879882812
C3 = TWO_PI - C1 - C2

COL_BMOD = 0
COL_N1 = COL_BMOD + NMT
COL_N2 = COL_N1 + KD
COL_NF = COL_N2 + KD
COL_BGLU = COL_NF + KD
COL_CW = COL_BGLU + KS
COL_CB = COL_CW + 3 * KS
COL_OG = COL_CB + KS
NCOL = COL_OG + KD


class Chain:

    def __init__(self, eng, sem, base=0, settle=False):
        self.eng, self.sem, self.n, self.base, self.settle = eng, sem, 0, base, settle

    def __call__(self, *instructions):
        for ins in instructions:
            self.n += 1
            ins.then_inc(self.sem, 1)
        self.eng.wait_ge(self.sem, self.n + self.base)
        if self.settle:
            self.eng.nop(nofuse=True)


def build(nc, xT, condT, cols, w_mod, w_u, w_tiles, ssm, bc, dskip, skT, w_query, table, y_out, st_out, kfull):
    ctx = ExitStack()
    with ctx:
        def sb(name, shape, dt=F32):
            return ctx.enter_context(nc.sbuf_tensor(name, shape, dt))

        def sem(name):
            return ctx.enter_context(nc.semaphore(name))

        bank = [ctx.enter_context(nc.psum_tensor(f"bank{i}", [P, 512], F32)) for i in range(8)]

        hT_r = sb("hT_r", [P, KD * T])
        x_r = sb("x_r", [P, KD * T])
        mix_r = sb("mix_r", [P, KD * T])
        r1 = sb("r1", [P, 17408])
        r2 = sb("r2", [P, 17408])

        hT = hT_r[:, :].rearrange("p (k t) -> p k t", k=KD)
        Y = hT_r[0:NCH, 0:Q * DS].rearrange("p (t c) -> p t c", t=Q)
        xt = x_r[:, :].rearrange("p (k t) -> p k t", k=KD)
        uc = x_r[0:NCH, 0:Q * DS].rearrange("p (g s c) -> p g s c", g=NG, s=Q)
        dsk = x_r[0:NCH, Q * DS:Q * DS + DS]
        BP = x_r[:, 0:4096].rearrange("p (r q s c) -> p r q s c", r=2, q=NPAIR, s=Q)
        mix = mix_r[:, :].rearrange("p (k t) -> p k t", k=KD)
        Ksb = mix_r[0:48, 0:NPAIR * NLAG * GC].rearrange("p (q x) -> p q x", q=NPAIR)
        Bb = mix_r[:, 3840:4864].rearrange("p (r q c) -> p r q c", r=2, q=NQ)
        cc_t = mix_r[:, 0:T]
        pr_t = mix_r[:, T:2 * T]
        cv_t = mix_r[:, 2 * T:3 * T]
        BPT = r1[:, 0:8192].rearrange("p (q r n) -> p q r n", q=NQ, r=2)
        CP = r1[:, 8192:17408].rearrange("p (r q j c) -> p r q j c", r=2, q=NQ, j=Q + 1)
        M = r1[:, 0:4096].rearrange("p (g x) -> p g x", g=NG)
        Hb = r1[:, 4096:4096 + NCH * 2 * NPAIR].rearrange("p (c r q) -> p c r q", c=NCH, r=2)
        wm = r2[:, 0:4096].rearrange("p (a k m) -> p a k m", a=2, k=KD)
        gT = r2[:, 0:KS * T].rearrange("p (k t) -> p k t", k=KS)
        wu = r2[:, 4096:8192].rearrange("p (k m) -> p k m", k=KD)
        U = r2[:, 4096:4096 + NG * NCH].rearrange("p (g c) -> p g c", g=NG)
        HH = r2[:, 8192:8192 + NCH * 64].rearrange("p (c r d q) -> p c r d q", c=NCH, r=2, d=2)
        HHs = r2[:, 8192:8192 + NCH * 64].rearrange("p (c r x) -> p c r x", c=NCH, r=2)
        bcs = r2[:, 8192:8192 + 2048].rearrange("p (v q c) -> p v q c", v=4, q=NQ)
        P9 = r2[:, 10240:10816].rearrange("p (j r q) -> p j r q", j=Q + 1, r=2)
        P9r = r2[:, 10816:11392].rearrange("p (j r q) -> p j r q", j=Q + 1, r=2)
        tp = r2[:, 11392:11968].rearrange("p (q j c) -> p q j c", q=4, j=Q + 1)
        tv = r2[:, 11968:12992].rearrange("p (q s c) -> p q s c", q=8, s=Q)
        wt = r2[:, 13312:15360].rearrange("p (a k m) -> p a k m", a=2, k=KD)
        rs = r2[:, 15360:15360 + T]
        sq = [r2[:, 16000:16000 + T], r2[:, 16640:16640 + T]]
        rows = r1[:, 0:SLOTS * 2 * D].rearrange("p (s x) -> p s x", s=SLOTS)
        wq = r2[:, 0:KD * 2048].rearrange("p (k m) -> p k m", k=KD)
        peer = r2[:, 16384:17408]

        def mx(a, n):
            return mix_r[:, a:a + n]
        h2Tc = mx(0, 1024).rearrange("p (k t) -> p k t", k=KD)
        h2c = mx(1024, 1024)
        q_s = mx(2048, 256)
        qT = mx(2304, 256).rearrange("p (h t) -> p h t", h=2)
        sc = mx(2560, 256).rearrange("p (h n) -> p h n", h=2)
        sc2 = mx(2816, 256).rearrange("p (h n) -> p h n", h=2)
        cand = mx(3072, 256)
        cand2 = mx(3328, 256)
        eq = mx(3584, 512)
        diag = mx(4096, 512).rearrange("p (a m) -> p a m", a=4)
        m16 = mx(4608, 32).rearrange("p (h n) -> p h n", h=2)
        i12 = mx(4640, 32).rearrange("p (h n) -> p h n", h=2)
        e16 = mx(4672, 16)
        top = mx(4688, 16)
        hid = mx(4704, 32).rearrange("p (a n) -> p a n", a=2)
        gel = mx(4736, 32).rearrange("p (a n) -> p a n", a=2)
        gate = mx(4768, 32).rearrange("p (a n) -> p a n", a=2)
        g2b = mx(4800, NBLK * KD).rearrange("p (b k) -> p b k", b=NBLK)

        idf = mx(4848, TOPK)

        ident = sb("ident", [P, P])
        ones = sb("ones", [P, P])
        zeros = sb("zeros", [P, P])
        headones = sb("headones", [P, P])
        iota = sb("iota", [P, TOPK])
        colv = sb("colv", [P, NCOL])
        cond = sb("cond", [P, KD, 2])
        modT = sb("modT", [P, NMT, 2])
        gs = sb("gs", [P, KD, 2])
        ssmv = sb("ssmv", [P, 5, NQ])
        sv = sb("sv", [P, 12, NQ])
        kint = sb("kint", [P, NQ], I32)
        AR = sb("AR", [P, 2, NQ])
        AI = sb("AI", [P, 2, NQ])
        fin = sb("fin", [P, 2, NQ])
        scan_a = sb("scan_a", [P, 2, NQ])
        scan_b = sb("scan_b", [P, 2, NQ])
        sk = sb("sk", [P, 2, NKEY])
        eps_c = sb("eps_c", [P, 1])
        frs = sb("frs", [P, P])
        small = sb("small", [P, 4])
        i16 = sb("i16", [P, 2, TOPK], U32)
        pos = sb("pos", [P, TOPK], U32)
        ab = sb("ab", [P, TOPK, 2], U32)
        gidx = sb("gidx", [P, 2, TOPK], U32)

        def col(a, n=1):
            return colv[:, a:a + n]

        ld_cond = sem("ld_cond")
        ld_ssm = sem("ld_ssm")
        ld_x = sem("ld_x")
        ld_x2 = sem("ld_x2")
        ld_wu = sem("ld_wu")
        ld_sk = sem("ld_sk")
        ld_dsk = sem("ld_dsk")
        ld_wq = sem("ld_wq")
        ld_wq2 = sem("ld_wq2")
        ld_m = sem("ld_m")
        wm_in = [sem(f"wm_in{i}") for i in range(2)]
        wt_in = [sem(f"wt_in{i}") for i in range(2)]
        row_in = [sem(f"row_in{i}") for i in range(SLOTS)]
        consts = sem("consts")
        silu_done = sem("silu_done")
        mod_mm = sem("mod_mm")
        mod_free = sem("mod_free")
        mod_ready = sem("mod_ready")
        bp_ready = sem("bp_ready")
        bpt_mm = sem("bpt_mm")
        bpt_ev = sem("bpt_ev")
        cp_ready = sem("cp_ready")
        p9_ready = sem("p9_ready")
        bb_ready = sem("bb_ready")
        ssm_act = sem("ssm_act")
        ssm_dve = sem("ssm_dve")
        k_mm = sem("k_mm")
        k_ev = sem("k_ev")
        k_out = sem("k_out")
        sq_ready = sem("sq_ready")
        sq_used = sem("sq_used")
        rms_act = sem("rms_act")
        xs_ready = sem("xs_ready")
        h_ready = sem("h_ready")
        u_mm = sem("u_mm")
        u_ev = sem("u_ev")
        ut_mm = sem("ut_mm")
        ut_ev = sem("ut_ev")
        ud_ready = sem("ud_ready")
        s_mm = sem("s_mm")
        s_ev = sem("s_ev")
        h0_set = sem("h0_set")
        scan_seq = sem("scan_seq")
        hb_ready = sem("hb_ready")
        z_mm = sem("z_mm")
        cc_ev = sem("cc_ev")
        ch_ev = sem("ch_ev")
        cb_ev = sem("cb_ev")
        conv_seq = sem("conv_seq")
        dve_seq = sem("dve_seq")
        act_seq = sem("act_seq")
        pool_seq = sem("pool_seq")
        y_mm = sem("y_mm")
        y_ev = sem("y_ev")
        y_gelu = sem("y_gelu")
        gt_mm = sem("gt_mm")
        gt_ev = sem("gt_ev")
        glu_mm = sem("glu_mm")
        glu_sig = sem("glu_sig")
        glu_ev = sem("glu_ev")
        mix_ready = sem("mix_ready")
        o_mm = sem("o_mm")
        x1_ready = sem("x1_ready")
        st_done = sem("st_done")
        h2_staged = sem("h2_staged")
        q_mm = sem("q_mm")
        q_ev = sem("q_ev")
        qt_mm = sem("qt_mm")
        qt_ev = sem("qt_ev")
        sc_mm = sem("sc_mm")
        sc_ev = sem("sc_ev")
        cand_ready = sem("cand_ready")
        exp_done = sem("exp_done")
        topk_done = sem("topk_done")
        topk_seq = sem("topk_seq")
        h2c_mm = sem("h2c_mm")
        h2c_ready = sem("h2c_ready")
        dot_done = sem("dot_done")
        gelu_done = sem("gelu_done")
        diag_ready = sem("diag_ready")
        diag_free = sem("diag_free")
        slot_free = sem("slot_free")
        v_done = sem("v_done")
        peer_ev = sem("peer_ev")
        pt_mm = sem("pt_mm")
        x2_ready = sem("x2_ready")
        fsq_ready = sem("fsq_ready")
        fs_mm = sem("fs_mm")
        frt = sem("frt")
        out_ready = sem("out_ready")
        out_dma = sem("out_dma")
        fin_seq = sem("fin_seq")
        st_dma = sem("st_dma")

        NM1 = 2 * KD // MCH
        NM2 = NMT // MCH - NM1
        NM_BODY = NM2 // KS
        assert NM2 % KS == 0 and NM_BODY == 4
        MOD_AT = [(), (0, 1), (2, 3)]
        NWT = 3 * KS + KS + KD
        RMS = 2 * KD

        block = ctx.enter_context(nc.Block())

        @block.sync
        def _(sp):
            w_mod_v = w_mod.rearrange("(k p) m -> p k m", p=P)
            CW = MCH * P
            sp.dma_start(cond[:, :, :], condT).then_inc(ld_cond, 16)
            sp.dma_start(colv[:, :], cols).then_inc(ld_cond, 16)
            sp.dma_start(ssmv[:, :, :], ssm).then_inc(ld_ssm, 16)
            sp.dma_start(bcs, bc).then_inc(ld_ssm, 16)
            for n in range(2):
                sp.dma_start(wm[:, n, :, :], w_mod_v[:, :, n * CW:(n + 1) * CW]).then_inc(wm_in[n], 16)
            sp.dma_start(hT, xT).then_inc(ld_x, 16)
            with nc.sync.Fori(1, NM1 // 2) as i:
                for a in range(2):
                    sp.wait_ge(mod_mm, i * 2 + a - 1)
                    sp.dma_start(wm[:, a, :, :], w_mod_v[:, :, bass.ds((i * 2 + a) * CW, CW)]).then_inc(wm_in[a], 16)
            sp.dma_start(wu, w_u).then_inc(ld_wu, 16)
            sp.dma_start(sk[:, :, :], skT).then_inc(ld_sk, 16)
            for n in range(2):
                sp.dma_start(wt[:, n, :, :], w_tiles[n]).then_inc(wt_in[n], 16)
            sp.wait_ge(bpt_mm, 16)
            sp.dma_start(dsk, dskip).then_inc(ld_dsk, 16)
            sp.wait_ge(k_ev, 8)
            kf = kfull.rearrange("(q a p) x -> a p q x", a=2, p=GC)
            for a in range(2):
                sp.dma_start(kf[a], Ksb[32 * a:32 * a + GC, :, :]).then_inc(k_out, 16)
            sp.wait_ge(s_mm, 16)
            sp.wait_ge(k_out, 32)
            kv = kfull.rearrange("(g p) x -> p g x", p=GC)
            for s in range(Q):
                sp.dma_start(M[s * GC:(s + 1) * GC, :, :], kv[:, :, (Q - 1 - s) * GC:(Q - 1 - s) * GC + P]).then_inc(ld_m, 16)

            def mod_load(i, j):
                sp.wait_ge(mod_mm, i * NM_BODY + (NM1 + j - 1))
                sp.dma_start(wm[:, j % 2, :, :],
                             w_mod_v[:, :, bass.ds((i * NM_BODY + (NM1 + j)) * CW, CW)]).then_inc(wm_in[j % 2], 16)

            with nc.sync.Fori(0, KS // 2) as i2:
                for e in range(2):
                    i = i2 * 2 + e
                    for r in range(3):
                        for j in MOD_AT[r]:
                            mod_load(i, j)
                        n = 3 * e + r
                        sp.wait_ge(z_mm, i * 3 + r + 1)
                        sp.dma_start(wt[:, n % 2, :, :],
                                     w_tiles[bass.ds(i * 3 + (r + 2), 1)].rearrange("a p k m -> p (a k) m")
                                     ).then_inc(wt_in[n % 2], 16)
            for n in range(3 * KS + 2, NWT):
                sp.wait_ge(z_mm, n - 1)
                sp.dma_start(wt[:, n % 2, :, :], w_tiles[n]).then_inc(wt_in[n % 2], 16)
                if n == 3 * KS + 2:
                    sp.wait_ge(y_ev, NG // 4)
                    sp.dma_start(xt, xT).then_inc(ld_x2, 16)
                if n == 4 * KS + 2:
                    sp.wait_ge(y_mm, 8)
                    sp.dma_start(st_out, fin[:, :, :]).then_inc(st_dma, 16)
                    for k in range(2, 6):
                        sp.dma_start(wq[:, k, :], w_query[:, k, :]).then_inc(ld_wq, 16)
            sp.wait_ge(z_mm, NWT)
            for k in (0, 1, 6, 7):
                if k == 7:
                    sp.wait_ge(h_ready, 2 * KD)
                sp.dma_start(wq[:, k, :], w_query[:, k, :]).then_inc(ld_wq, 16)
            with nc.sync.Fori(0, NBLK) as b:
                sp.wait_ge(out_ready, b + 1)
                sp.dma_start(y_out[:, :, bass.ds(b * P, P)], peer.rearrange("p (k t) -> p k t", k=KD)).then_inc(out_dma, 16)
            sp.wait_ge(out_dma, 16 * NBLK)
            sp.wait_ge(st_dma, 16)
            sp.wait_ge(k_out, 32)

        @block.tensor
        def _(pe):
            mm = nc.tensor.matmul

            def mod_step(turn, chunk, a):
                pe.wait_ge(wm_in[a], turn * 16 + 16)
                pe.wait_ge(mod_free, chunk + 1)
                for m in range(MCH):
                    for k in range(KD):
                        last = mm(bank[6 + a][:, 2 * m:2 * m + 2], wm[:, a, k, m * P:(m + 1) * P],
                                  cond[:, k, :], start=(k == 0), stop=(k == KD - 1))
                last.then_inc(mod_mm, 1)

            pe.wait_ge(silu_done, 1)
            with nc.tensor.Fori(0, NM1 // 2) as i:
                for a in range(2):
                    mod_step(i, i * 2 + a, a)

            def sum_squares(first, count, b0, b1, group=None):
                for k in range(count):
                    pe.wait_ge(sq_ready, first + k + 1)
                    w = ones if group is None else headones
                    alone = group is not None
                    mm(bank[b0][:, :], w[:, :], sq[(first + k) % 2][:, CTX:T], start=(k == 0 or alone), stop=(k == count - 1 or alone))
                    last = mm(bank[b1][:, 0:CTX], w[:, :], sq[(first + k) % 2][:, 0:CTX], start=(k == 0 or alone), stop=(k == count - 1 or alone))
                    last.then_inc(sq_used, 1)

            def turn_inputs(d):
                pe.wait_ge(bp_ready, d + 1)
                for g in range(8 * d, 8 * d + 8):
                    q0 = (g % 8) * 2
                    if g >= 2:
                        pe.wait_ge(bpt_ev, g - 1)
                    for j in range(4):
                        src = BP[:, j % 2, q0 + j // 2, :, :].rearrange("p s c -> p (s c)")
                        last = nc.tensor.transpose(bank[g % 2][:, j * P:(j + 1) * P], src, ident[:, :])
                    last.then_inc(bpt_mm, 1)

            pe.wait_ge(consts, 1)
            turn_inputs(0)
            sum_squares(0, KD, 4, 5)
            turn_inputs(1)

            pe.wait_ge(ld_wu, 16)
            pe.wait_ge(h_ready, KD)
            for s in range(Q):
                if s >= 2:
                    pe.wait_ge(u_ev, s - 1)
                else:
                    pe.wait_ge(bpt_ev, 15 + s)
                for k in range(KD):
                    last = mm(bank[s % 2][0:NCH, :], hT[:, k, s:T:Q], wu[:, k, :], start=(k == 0), stop=(k == KD - 1))
                last.then_inc(u_mm, 1)
            pe.wait_ge(u_ev, Q)
            for g4 in range(NG // 4):
                if g4 >= 2:
                    pe.wait_ge(ut_ev, g4 - 1)
                for j in range(4):
                    g = 4 * g4 + j
                    last = nc.tensor.transpose(bank[2 + g4 % 2][:, j * NCH:(j + 1) * NCH], uc[:, g, :, :].rearrange("p s c -> p (s c)"), ident[0:NCH, 0:NCH])
                last.then_inc(ut_mm, 1)
            pe.wait_ge(ut_ev, NG // 4)
            pe.wait_ge(bpt_ev, 16)
            for g in range(16):
                if g >= 2:
                    pe.wait_ge(s_ev, g - 1)
                for j in range(2):
                    q = 2 * g + j
                    for r in range(2):
                        for a in range(2):
                            last = mm(bank[4 + g % 2][64 * a:64 * a + 64, (2 * j + r) * NCH:(2 * j + r + 1) * NCH],
                                      BPT[:, q, r, 64 * a:64 * a + 64], U[:, 2 * (q % NPAIR) + a, :], start=True, stop=True)
                last.then_inc(s_mm, 1)

            pe.wait_ge(bb_ready, 1)
            pe.wait_ge(cp_ready, 1)
            for g in range(8):
                d = g // 4
                if g >= 2:
                    pe.wait_ge(k_ev, g - 1)
                for j in range(4):
                    q = d * NPAIR + (g % 4) * 4 + j
                    for a in range(2):
                        for r in range(2):
                            rhs = CP[64 * a:64 * a + 64, r, q, d:d + Q, :].rearrange("p j c -> p (j c)")
                            last = mm(bank[2 + g % 2][32 * a:32 * a + GC, j * P:(j + 1) * P],
                                      Bb[64 * a:64 * a + 64, r, q, :], rhs, start=(r == 0), stop=(r == 1))
                last.then_inc(k_mm, 1)

            def tile(slot, turn, kt, src, b0, half):
                pe.wait_ge(wt_in[slot], turn)
                for k in range(kt):
                    mm(bank[b0][:, :], wt[:, slot, k, :], src[:, k, CTX:T], start=(k == 0), stop=(k == kt - 1))
                for k in range(kt):
                    last = mm(half, wt[:, slot, k, :], src[:, k, 0:CTX], start=(k == 0), stop=(k == kt - 1))
                last.then_inc(z_mm, 1)

            pe.wait_ge(k_ev, 8)
            pe.wait_ge(s_ev, 16)
            with nc.tensor.Fori(0, KS // 2) as i2:
                for e in range(2):
                    i = i2 * 2 + e
                    for r in range(3):
                        for j in MOD_AT[r]:
                            mod_step(i * (NM_BODY // 2) + (NM1 // 2 + j // 2), i * NM_BODY + (NM1 + j), j % 2)
                        pe.wait_ge((cc_ev, ch_ev, cb_ev)[r], i)
                        n = 3 * e + r
                        tile(n % 2, i2 * 48 + (n // 2 + 1) * 16, KD, hT, r, bank[3 + r][:, 0:CTX])

            pe.wait_ge(ld_m, 16 * Q)
            pe.wait_ge(hb_ready, 2)
            pe.wait_ge(cb_ev, KS)
            for g4 in range(NG // 4):
                if g4 >= 2:
                    pe.wait_ge(y_ev, g4 - 1)
                a = g4 % 2
                for j in range(4):
                    pr = 4 * (g4 // 2) + j
                    g = 2 * pr + a
                    out = bank[4 + g4 % 2][0:NCH, j * P:(j + 1) * P]
                    mm(out, U[:, g, :], M[:, g, :], start=True, stop=False)
                    rows_a = slice(64 * a, 64 * a + 64)
                    for r in range(2):
                        mm(out, HH[rows_a, :, r, 0, pr], CP[rows_a, r, pr, 1:Q + 1, :].rearrange("p j c -> p (j c)"),
                           start=False, stop=False)
                        last = mm(out, Hb[rows_a, :, r, pr], CP[rows_a, r, NPAIR + pr, 0:Q, :].rearrange("p j c -> p (j c)"),
                                  start=False, stop=(r == 1))
                last.then_inc(y_mm, 1)
            pe.wait_ge(y_gelu, 1)
            pe.wait_ge(mod_free, NMT // MCH + 2)
            for n in range(2 * KS):
                cb_, th = n // 2, n % 2
                if n >= 2:
                    pe.wait_ge(gt_ev, n - 1)
                for j in range(4):
                    last = nc.tensor.transpose(bank[6 + n % 2][:, j * NCH:(j + 1) * NCH],
                                               Y[:, 4 * th + j, cb_ * P:(cb_ + 1) * P], ident[0:NCH, 0:NCH])
                last.then_inc(gt_mm, 1)
            pe.wait_ge(gt_ev, 2 * KS)
            for m in range(KS):
                if m >= 2:
                    pe.wait_ge(glu_sig, 2 * (m - 1))
                n = 3 * KS + m
                tile(n % 2, (n // 2 + 1) * 16, KS, gT, m % 2, bank[2 + m % 2][:, 0:CTX])
            sum_squares(KD, KS, 4, 5)
            for m in range(KS):
                if m >= 1:
                    pe.wait_ge(rms_act, 2 * (2 + m))
                sum_squares(KD + KS + m, 1, 6, 7, group=m)
            pe.wait_ge(mix_ready, KD)
            pe.wait_ge(glu_sig, 2 * KS)
            for m in range(KD):
                if m >= 2:
                    pe.wait_ge(x1_ready, 2 * (m - 1))
                n = 4 * KS + m
                tile(n % 2, (n // 2 + 1) * 16, KD, mix, m % 2, bank[2 + m % 2][:, 0:CTX])
            sum_squares(KD + 2 * KS, KD, 4, 5)

            def query(t, col0):
                pe.wait_ge(h2_staged, t + 1)
                for k in range(KD):
                    last = mm(bank[2][:, 0:DQ], h2Tc[:, k, :], wq[:, k, bass.ds(col0, DQ)], start=(k == 0), stop=(k == KD - 1))
                last.then_inc(q_mm, 1)

            def query_turn(t):
                pe.wait_ge(q_ev, t + 1)
                for h in range(2):
                    last = nc.tensor.transpose(bank[3][:, h * P:(h + 1) * P], q_s[:, h * P:(h + 1) * P], ident[:, :])
                last.then_inc(qt_mm, 1)

            def scores(t):
                pe.wait_ge(qt_ev, t + 1)
                for h in range(2):
                    last = mm(bank[6][:, h * P:(h + 1) * P], qT[:, h, :], sk[:, h, :], start=True, stop=True)
                last.then_inc(sc_mm, 1)

            def add_rows(n, k):
                pe.wait_ge(diag_ready, n + k + 1)
                for h in range(2):
                    last = mm(bank[h][:, :], diag[:, k % 4, :], rows[:, k % SLOTS, D + h * 512:D + (h + 1) * 512],
                              start=False, stop=False, skip_group_check=True)
                last.then_inc(v_done, 1)

            pe.wait_ge(ld_wq, 16 * KD)
            pe.wait_ge(ld_sk, 16)
            pe.wait_ge(x1_ready, 2 * KD)
            query(0, 0)
            query_turn(0)
            scores(0)
            with nc.tensor.Fori(0, NBLK) as b:
                for k in range(KD):
                    last = nc.tensor.transpose(bank[4 + k // 4][:, (k % 4) * P:(k % 4 + 1) * P], h2Tc[:, k, :], ident[:, :])
                last.then_inc(h2c_mm, 1)
                pe.wait_ge(peer_ev, b)
                for h in range(2):
                    for j in range(4):
                        mm(bank[h][:, j * P:(j + 1) * P], zeros[:, :], zeros[:, :], start=(j == 0), stop=False, skip_group_check=True)
                with nc.tensor.Fori(0, HEADS // 2) as hp:
                    for e in range(2):
                        G = b * HEADS + hp * 2 + e
                        t = G + 1
                        query(t, (t % HEADS) * DQ)
                        add_rows(G * TOPK, 0)
                        query_turn(t)
                        add_rows(G * TOPK, 1)
                        scores(t)
                        for k in range(2, TOPK):
                            add_rows(G * TOPK, k)
                pe.wait_ge(peer_ev, b + 1)
                for k in range(KD):
                    last = nc.tensor.transpose(bank[4 + k // 4][:, (k % 4) * P:(k % 4 + 1) * P], peer[:, k * P:(k + 1) * P], ident[:, :])
                last.then_inc(pt_mm, 1)
                pe.wait_ge(fsq_ready, b + 1)
                for k in range(KD):
                    last = mm(bank[7][:, 0:P], ones[:, :], peer[:, k * P:(k + 1) * P], start=(k == 0), stop=(k == KD - 1))
                last.then_inc(fs_mm, 1)

        @block.scalar
        def _(act):
            A = nc.scalar.activation
            link = Chain(act, act_seq)
            act.wait_ge(ld_cond, 32)
            A(cond[:, :, :], cond[:, :, :], ACT.Silu).then_inc(silu_done, 1)
            act.wait_ge(ld_ssm, 32)
            A(sv[:, 0, :], ssmv[:, 2, :], ACT.Exp).then_inc(ssm_act, 1)
            act.wait_ge(ssm_dve, 1)
            A(sv[:, 3, :], sv[:, 1, :], ACT.Exp).then_inc(ssm_act, 1)
            act.wait_ge(ssm_dve, 2)
            A(sv[:, 6, :], sv[:, 4, :], ACT.Sin).then_inc(ssm_act, 1)
            A(sv[:, 7, :], sv[:, 5, :], ACT.Sin).then_inc(ssm_act, 1)

            act.sem_inc(mod_free, 2)

            def mod_take(chunk, a):
                act.wait_ge(mod_mm, chunk + 1)
                for m in range(MCH):
                    at = chunk * MCH + m
                    last = A(modT[:, bass.ds(at, 1), :].rearrange("p a c -> p (a c)"), bank[6 + a][:, 2 * m:2 * m + 2],
                             ACT.Identity, bias=colv[:, bass.ds(at + COL_BMOD, 1)])
                last.then_inc(mod_free, 1)

            with nc.scalar.Fori(0, NM1 // 2) as i:
                for a in range(2):
                    mod_take(i * 2 + a, a)

            def take_inputs(d):
                for g in range(8 * d, 8 * d + 8):
                    act.wait_ge(bpt_mm, g + 1)
                    A(BPT[:, 2 * g:2 * g + 2, :, :].rearrange("p q r n -> p (q r n)"), bank[g % 2][:, :], ACT.Copy).then_inc(bpt_ev, 1)

            take_inputs(0)

            def squares(src, first, count, parts=1):
                for k in range(count):
                    if first + k >= 2:
                        act.wait_ge(sq_used, first + k - 1)
                    A(sq[(first + k) % 2], src(k), ACT.Square).then_inc(sq_ready, 1)

            def roots(used, b0, b1, width, turn):
                act.wait_ge(sq_used, used)
                if turn:
                    act.wait_ge(xs_ready, turn)
                A(rs[:, CTX:T], bank[b0][:, :], ACT.Sqrt, scale=1.0 / width, bias=eps_c[:, 0:1]).then_inc(rms_act, 1)
                A(rs[:, 0:CTX], bank[b1][:, 0:CTX], ACT.Sqrt, scale=1.0 / width, bias=eps_c[:, 0:1]).then_inc(rms_act, 1)

            def modulate(shift, first):
                for k in range(KD):
                    act.wait_ge(xs_ready, first + k + 1)
                    A(hT[:, k, 0:CTX], hT[:, k, 0:CTX], ACT.Identity, scale=gs[:, k, 0:1],
                      bias=modT[:, shift * KD + k, 0:1])
                    A(hT[:, k, CTX:T], hT[:, k, CTX:T], ACT.Identity, scale=gs[:, k, 1:2],
                      bias=modT[:, shift * KD + k, 1:2]).then_inc(h_ready, 1)

            act.wait_ge(consts, 1)
            act.wait_ge(ld_x, 16)
            squares(lambda k: hT[:, k, :], 0, KD)
            roots(KD, 4, 5, D, 0)
            act.wait_ge(mod_ready, 1)
            modulate(0, 0)
            take_inputs(1)
            for s in range(Q):
                act.wait_ge(u_mm, s + 1)
                if s == 0:
                    act.wait_ge(bpt_mm, 16)
                A(uc[:, :, s, :], bank[s % 2][0:NCH, :].rearrange("p (g c) -> p g c", g=NG), ACT.Copy).then_inc(u_ev, 1)
            for g4 in range(NG // 4):
                act.wait_ge(ut_mm, g4 + 1)
                A(U[:, 4 * g4:4 * g4 + 4, :].rearrange("p g c -> p (g c)"), bank[2 + g4 % 2][:, 0:4 * NCH], ACT.Copy).then_inc(ut_ev, 1)
            act.wait_ge(cp_ready, 1)
            act.wait_ge(bp_ready, 2)
            for g in range(16):
                d, pr = g // 8, (g % 8) * 2
                act.wait_ge(s_mm, g + 1)
                for r in range(2):
                    src = bank[4 + g % 2][:, 0:4 * NCH].rearrange("p (q r c) -> p c r q", q=2, r=2)[:, :, r, :]
                    if d == 0:
                        last = A(HH[:, 1:NCH, r, 0, pr:pr + 2], src[:, 0:NCH - 1, :], ACT.Copy)
                    else:
                        A(HH[:, NCC:0:-1, r, 1, pr:pr + 2], src[:, 0:NCC, :], ACT.Copy)
                        last = A(HH[:, NCH - 1:NCC:-1, r, 1, pr:pr + 2], src[:, NCC + 1:NCH, :], ACT.Copy)
                last.then_inc(s_ev, 1)
            act.wait_ge(k_out, 32)
            with nc.scalar.Fori(0, KS) as i:
                act.wait_ge(z_mm, i * 3 + 1)
                act.wait_ge(ch_ev, i)
                A(cc_t[:, CTX:T], bank[0][:, :], ACT.Copy)
                A(cc_t[:, 0:CTX], bank[3][:, 0:CTX], ACT.Copy).then_inc(cc_ev, 1)
                for j in range(NM_BODY):
                    mod_take(i * NM_BODY + (NM1 + j), j % 2)
            act.wait_ge(scan_seq, 1)
            A(Hb[:, 0:NCC, :, :], HH[:, NCC - 1::-1, :, 1, :], ACT.Copy).then_inc(hb_ready, 1)
            A(Hb[:, NCC:NCH, :, :], HH[:, NCH - 1:NCC - 1:-1, :, 1, :], ACT.Copy).then_inc(hb_ready, 1)
            act.wait_ge(y_ev, NG // 4)
            A(Y[:, :, :], Y[:, :, :], ACT.Gelu_apprx_tanh).then_inc(y_gelu, 1)
            for n in range(2 * KS):
                act.wait_ge(gt_mm, n + 1)
                cb_, th = n // 2, n % 2
                A(gT[:, cb_, :].rearrange("p (c t) -> p t c", t=Q)[:, 4 * th:4 * th + 4, :],
                  bank[6 + n % 2][:, 0:4 * NCH].rearrange("p (t c) -> p t c", t=4), ACT.Copy).then_inc(gt_ev, 1)
            for m in range(KS):
                act.wait_ge(z_mm, 3 * KS + m + 1)
                A(mix[:, m, CTX:T], bank[m % 2][:, :], ACT.Sigmoid, bias=col(COL_BGLU + m)).then_inc(glu_sig, 1)
                A(mix[:, m, 0:CTX], bank[2 + m % 2][:, 0:CTX], ACT.Sigmoid, bias=col(COL_BGLU + m)).then_inc(glu_sig, 1)
            act.wait_ge(glu_ev, KS)
            squares(lambda k: mix[:, k, :], KD, KS)
            roots(KD + KS, 4, 5, DS, KD)
            for m in range(KS):
                squares(lambda k: mix[:, KS + m, :], KD + KS + m, 1)
                roots(KD + KS + m + 1, 6, 7, DC // 8, KD + (1 if m == 0 else 1 + m))
            act.wait_ge(x1_ready, 2 * KD)
            squares(lambda k: xt[:, k, :], KD + 2 * KS, KD)
            roots(2 * KD + 2 * KS, 4, 5, D, KD + 1 + KS)
            act.wait_ge(mod_ready, 2)
            modulate(3, KD + 1 + KS)

            def stage(t, blk):
                act.wait_ge(q_mm, t)
                A(h2Tc[:, :, :], hT[:, :, bass.ds(blk * P, P)], ACT.Copy).then_inc(h2_staged, 1)

            def take_q(t):
                act.wait_ge(q_mm, t + 1)
                A(q_s, bank[2][:, 0:DQ], ACT.Copy).then_inc(q_ev, 1)

            def take_qt(t):
                act.wait_ge(qt_mm, t + 1)
                A(qT.rearrange("p h t -> p (h t)"), bank[3][:, 0:DQ], ACT.Copy).then_inc(qt_ev, 1)

            def take_scores(t):
                act.wait_ge(sc_mm, t + 1)
                A(sc.rearrange("p h t -> p (h t)"), bank[6][:, 0:DQ], ACT.Copy).then_inc(sc_ev, 1)

            def exps(t):
                act.wait_ge(cand_ready, t + 1)
                A(e16, top, ACT.Exp, bias=small[:, 0:1], accum_out=small[:, 1:2]).then_inc(exp_done, 1)

            def gelu(G, par, k):
                act.wait_ge(dot_done, G * TOPK + (k + 1))
                A(gel[:, par, k:k + 1], hid[:, par, k:k + 1], ACT.Gelu_apprx_tanh).then_inc(gelu_done, 1)

            act.wait_ge(h_ready, 2 * KD)
            A(h2Tc[:, :, :], hT[:, :, 0:P], ACT.Copy).then_inc(h2_staged, 1)
            take_q(0)
            take_qt(0)
            take_scores(0)
            exps(0)
            with nc.scalar.Fori(0, NBLK) as b:
                act.wait_ge(h2c_mm, b + 1)
                A(h2c[:, 0:512], bank[4][:, :], ACT.Copy)
                A(h2c[:, 512:1024], bank[5][:, :], ACT.Copy).then_inc(h2c_ready, 1)
                with nc.scalar.Fori(0, HEADS // 2) as hp:
                    for e in range(2):
                        G = b * HEADS + hp * 2 + e
                        t = G + 1
                        stage(t, (t // HEADS) % NBLK)
                        gelu(G, e, 0)
                        take_q(t)
                        gelu(G, e, 1)
                        take_qt(t)
                        gelu(G, e, 2)
                        take_scores(t)
                        gelu(G, e, 3)
                        gelu(G, e, 4)
                        exps(t)
                        for k in range(5, TOPK):
                            gelu(G, e, k)
                act.wait_ge(v_done, b * (HEADS * TOPK) + (HEADS * TOPK + SLOTS))
                act.wait_ge(out_dma, b * 16)
                A(peer[:, 0:512], bank[0][:, :], ACT.Copy)
                A(peer[:, 512:1024], bank[1][:, :], ACT.Copy).then_inc(peer_ev, 1)
                act.wait_ge(x2_ready, b + 1)
                A(peer.rearrange("p (k t) -> p k t", k=KD), xt[:, :, bass.ds(b * P, P)], ACT.Square).then_inc(fsq_ready, 1)
                act.wait_ge(fs_mm, b + 1)
                A(frs[:, :], bank[7][:, 0:P], ACT.Sqrt, scale=1.0 / D, bias=eps_c[:, 0:1]).then_inc(frt, 1)

        @block.vector
        def _(dve):
            V = nc.vector
            link = Chain(dve, dve_seq)
            tt, ts, stt = V.tensor_tensor, V.tensor_scalar, V.scalar_tensor_tensor
            dve.wait_ge(ld_ssm, 32)
            dve.wait_ge(ssm_act, 1)
            lre, lim, dt = ssmv[:, 0, :], ssmv[:, 1, :], sv[:, 0, :]
            tt(sv[:, 1, :], lre, dt, ALU.mult).then_inc(ssm_dve, 1)
            link(tt(sv[:, 2, :], lim, dt, ALU.mult))
            link(ts(sv[:, 8, :], sv[:, 2, :], 1.0 / TWO_PI, None, ALU.mult))
            link(V.tensor_copy(kint[:, :], sv[:, 8, :]))
            link(V.tensor_copy(sv[:, 8, :], kint[:, :]))
            link(stt(sv[:, 4, :], sv[:, 8, :], -C1, sv[:, 2, :], ALU.mult, ALU.add))
            link(stt(sv[:, 4, :], sv[:, 8, :], -C2, sv[:, 4, :], ALU.mult, ALU.add))
            link(stt(sv[:, 4, :], sv[:, 8, :], -C3, sv[:, 4, :], ALU.mult, ALU.add))
            link(ts(sv[:, 5, :], sv[:, 4, :], TWO_PI / 4, None, ALU.add))
            link(ts(sv[:, 9, :], sv[:, 5, :], TWO_PI / 2, -TWO_PI, ALU.is_gt, ALU.mult))
            link(tt(sv[:, 5, :], sv[:, 5, :], sv[:, 9, :], ALU.add))
            link(ts(sv[:, 5, :], sv[:, 5, :], PI_IN, -PI_IN, ALU.min, ALU.max))
            ts(sv[:, 4, :], sv[:, 4, :], PI_IN, -PI_IN, ALU.min, ALU.max).then_inc(ssm_dve, 1)
            dve.wait_ge(ssm_act, 4)

            def cmul(o, a, b, t, n=None):
                link(tt(o[0], a[0], b[0], ALU.mult), tt(t, a[1], b[1], ALU.mult))
                link(tt(o[0], o[0], t, ALU.subtract))
                link(tt(o[1], a[0], b[1], ALU.mult), tt(t, a[1], b[0], ALU.mult))
                link(tt(o[1], o[1], t, ALU.add))

            link(V.memset(P9[:, 0, 0, :], 1.0), V.memset(P9[:, 0, 1, :], 0.0))
            link(tt(P9[:, 1, 0, :], sv[:, 3, :], sv[:, 7, :], ALU.mult),
                 tt(P9[:, 1, 1, :], sv[:, 3, :], sv[:, 6, :], ALU.mult))
            n = 1
            while n < Q:
                o = [P9[:, n + 1:2 * n + 1, r, :] for r in range(2)]
                x = [P9[:, n:n + 1, r, :].broadcast_to([P, n, NQ]) for r in range(2)]
                y = [P9[:, 1:n + 1, r, :] for r in range(2)]
                cmul(o, x, y, sv[:, 8:8 + n, :])
                n *= 2
            for j in range(Q + 1):
                last = V.tensor_copy(P9r[:, j, :, :], P9[:, Q - j, :, :])
                link(last)
            link(V.tensor_copy(AR[:, 0, :], P9[:, Q, 0, :]), V.tensor_copy(AR[:, 1, :], P9[:, Q, 0, :]),
                 V.tensor_copy(AI[:, 1, :], P9[:, Q, 1, :]), ts(AI[:, 0, :], P9[:, Q, 1, :], -1.0, None, ALU.mult))
            V.tensor_copy(sv[:, 11, :], sv[:, 3, :]).then_inc(p9_ready, 1)
            link(ts(sv[:, 0, :], P9[:, 1, 0, :], -1.0, None, ALU.add))
            link(tt(sv[:, 1, :], lre, lre, ALU.mult), tt(sv[:, 2, :], lim, lim, ALU.mult))
            link(tt(sv[:, 1, :], sv[:, 1, :], sv[:, 2, :], ALU.add))
            link(V.reciprocal(sv[:, 2, :], sv[:, 1, :]))
            im = P9[:, 1, 1, :]
            link(tt(sv[:, 4, :], sv[:, 0, :], lre, ALU.mult), tt(sv[:, 5, :], im, lim, ALU.mult))
            link(tt(sv[:, 4, :], sv[:, 4, :], sv[:, 5, :], ALU.add))
            link(tt(sv[:, 6, :], im, lre, ALU.mult), tt(sv[:, 7, :], sv[:, 0, :], lim, ALU.mult))
            link(tt(sv[:, 6, :], sv[:, 6, :], sv[:, 7, :], ALU.subtract))
            link(tt(sv[:, 4, :], sv[:, 4, :], sv[:, 2, :], ALU.mult), tt(sv[:, 6, :], sv[:, 6, :], sv[:, 2, :], ALU.mult))
            cf = [sv[:, v, :].rearrange("p (q a) -> p q a", a=1).broadcast_to([P, NQ, GC]) for v in (4, 6)]
            tb = tv.rearrange("p q s c -> p (q s c)")[:, 0:NQ * GC].rearrange("p (q c) -> p q c", q=NQ)
            cmul([Bb[:, 0, :, :], Bb[:, 1, :, :]], cf, [bcs[:, 0, :, :], bcs[:, 1, :, :]], tb)
            V.tensor_copy(sv[:, 10, :], sv[:, 4, :]).then_inc(bb_ready, 1)

            def chunk_inputs(d):
                w = P9r[:, 1:Q + 1] if d == 0 else P9[:, 0:Q]
                for h in range(2):
                    q = slice(d * NPAIR + 8 * h, d * NPAIR + 8 * h + 8)
                    pw = [w[:, :, r, q].rearrange("p s (q a) -> p q s a", a=1).broadcast_to([P, 8, Q, GC]) for r in range(2)]
                    bb = [Bb[:, r, q, :].rearrange("p q (a c) -> p q a c", a=1).broadcast_to([P, 8, Q, GC]) for r in range(2)]
                    cmul([BP[:, r, 8 * h:8 * h + 8, :, :] for r in range(2)], pw, bb, tv)
                V.tensor_copy(sv[:, 9, :], sv[:, 4, :]).then_inc(bp_ready, 1)

            chunk_inputs(0)

            def gains(sc_at, g_at, turn):
                dve.wait_ge(mod_free, turn)
                g = colv[:, g_at:g_at + KD].rearrange("p (k a) -> p k a", a=1).broadcast_to([P, KD, 2])
                stt(gs[:, :, :], modT[:, sc_at * KD:(sc_at + 1) * KD, :], 1.0, g, ALU.add, ALU.mult).then_inc(mod_ready, 1)

            def unroot(call):
                dve.wait_ge(rms_act, 2 * call + 2)
                link(V.reciprocal(rs, rs))

            gains(1, COL_N1, NM1 + 2)
            dve.wait_ge(ld_x, 16)
            unroot(0)
            for k in range(KD):
                tt(hT[:, k, :], hT[:, k, :], rs, ALU.mult).then_inc(xs_ready, 1)
            dve.wait_ge(bpt_mm, 8)
            chunk_inputs(1)
            dve.wait_ge(ld_dsk, 16)
            dve.wait_ge(ut_mm, NG // 4)
            tt(uc, uc, dsk.rearrange("p (g a c) -> p g a c", g=NG, a=1).broadcast_to([NCH, NG, Q, GC]), ALU.mult).then_inc(ud_ready, 1)
            for g in range(8):
                d, q4 = g // 4, slice((g % 4) * 4, (g % 4) * 4 + 4)
                dve.wait_ge(k_mm, g + 1)
                for a in range(2):
                    src = bank[2 + g % 2][32 * a:32 * a + GC, :].rearrange("p (q x) -> p q x", q=4)
                    dst = Ksb[32 * a:32 * a + GC, q4, :]
                    zero = (Q - 1) * GC
                    if d == 0:
                        last = V.tensor_copy(dst[:, :, zero:], src)
                    else:
                        link(V.tensor_copy(dst[:, :, 0:zero], src[:, :, 0:zero]))
                        last = tt(dst[:, :, zero:zero + GC], dst[:, :, zero:zero + GC], src[:, :, zero:], ALU.add)
                    if a == 0:
                        link(last)
                last.then_inc(k_ev, 1)
                dve.wait_ge(k_ev, g + 1)

            dve.wait_ge(k_out, 32)
            STEP = 12
            with nc.vector.Fori(0, KS) as i:
                cl = Chain(dve, conv_seq, i * STEP)
                w = [colv[:, bass.ds(i + (COL_CW + tap * KS), 1)] for tap in range(3)]
                dve.wait_ge(cc_ev, i + 1)
                dve.wait_ge(z_mm, i * 3 + 2)
                cl(tt(pr_t[:, CTX:T], cc_t[:, CTX:T], bank[1][:, :], ALU.mult))
                tt(pr_t[:, 0:CTX], cc_t[:, 0:CTX], bank[4][:, 0:CTX], ALU.mult).then_inc(ch_ev, 1)
                dve.wait_ge(ch_ev, i + 1)
                cl(ts(cv_t, pr_t, w[1], colv[:, bass.ds(i + COL_CB, 1)], ALU.mult, ALU.add))
                for lo, hi, rw in ((0, CTX, CTX), (CTX, T, ROW_W)):
                    pv = pr_t[:, lo:hi].rearrange("p (r w) -> p r w", w=rw)
                    cv = cv_t[:, lo:hi].rearrange("p (r w) -> p r w", w=rw)
                    cl(stt(cv[:, :, 1:rw], pv[:, :, 0:rw - 1], w[0], cv[:, :, 1:rw], ALU.mult, ALU.add))
                    cl(stt(cv[:, :, 0:rw - 1], pv[:, :, 1:rw], w[2], cv[:, :, 0:rw - 1], ALU.mult, ALU.add))
                dve.wait_ge(z_mm, i * 3 + 3)
                out = mix[:, bass.ds(i + KS, 1), :].rearrange("p a t -> p (a t)")
                cl(tt(out[:, CTX:T], cv_t[:, CTX:T], bank[2][:, :], ALU.mult))
                while cl.n < STEP:
                    cl(tt(small[:, 2:3], eps_c[:, :], eps_c[:, :], ALU.mult))
                tt(out[:, 0:CTX], cv_t[:, 0:CTX], bank[5][:, 0:CTX], ALU.mult).then_inc(cb_ev, 1)
                dve.wait_ge(cb_ev, i + 1)

            for g4 in range(NG // 4):
                dve.wait_ge(y_mm, g4 + 1)
                for j in range(4):
                    g = 2 * (4 * (g4 // 2) + j) + g4 % 2
                    cj = slice(g * GC, (g + 1) * GC)
                    last = tt(Y[:, :, cj], bank[4 + g4 % 2][0:NCH, j * P:(j + 1) * P].rearrange("p (t c) -> p t c", t=Q),
                              uc[:, g, :, :], ALU.add)
                last.then_inc(y_ev, 1)
            for m in range(KS):
                dve.wait_ge(glu_sig, 2 * (m + 1))
                dve.wait_ge(gt_ev, 2 * KS)
                tt(mix[:, m, :], mix[:, m, :], gT[:, m, :], ALU.mult).then_inc(glu_ev, 1)
            unroot(1)
            for m in range(KS):
                last = stt(mix[:, m, :], mix[:, m, :], col(COL_OG + m), rs, ALU.mult, ALU.mult)
                last.then_inc(mix_ready, 1)
            V.tensor_copy(small[:, 2:3], eps_c[:, :]).then_inc(xs_ready, 1)
            for m in range(KS):
                unroot(2 + m)
                stt(mix[:, KS + m, :], mix[:, KS + m, :], col(COL_OG + KS + m), rs, ALU.mult, ALU.mult).then_inc(mix_ready, 1)
                dve.wait_ge(mix_ready, KS + m + 1)
                V.tensor_copy(small[:, 2:3], eps_c[:, :]).then_inc(xs_ready, 1)
            dve.wait_ge(ld_x2, 16)
            dve.wait_ge(mod_free, NMT // MCH + 2)
            for m in range(KD):
                dve.wait_ge(z_mm, 4 * KS + m + 1)
                g1 = modT[:, 2 * KD + m, :]
                stt(xt[:, m, CTX:T], bank[m % 2][:, :], g1[:, 1:2], xt[:, m, CTX:T], ALU.mult, ALU.add).then_inc(x1_ready, 1)
                stt(xt[:, m, 0:CTX], bank[2 + m % 2][:, 0:CTX], g1[:, 0:1], xt[:, m, 0:CTX], ALU.mult, ALU.add).then_inc(x1_ready, 1)
            dve.wait_ge(h_ready, KD)
            gains(4, COL_N2, NMT // MCH + 2)
            unroot(2 + KS)
            for k in range(KD):
                tt(hT[:, k, :], xt[:, k, :], rs, ALU.mult).then_inc(xs_ready, 1)
            for b in range(NBLK):
                last = V.tensor_copy(g2b[:, b, :], modT[:, 5 * KD:6 * KD, min(b, 1)])
            link(last)

            NT = 40

            def topk_keys(cl, t):
                dve.wait_ge(sc_ev, t + 1)
                dve.nop(nofuse=True)
                cl(*[V.max(m16[:, h, 0:8], sc[:, h, :]) for h in range(2)])
                cl(*[V.max_index(i16[:, h, 0:8], m16[:, h, 0:8], sc[:, h, :]) for h in range(2)],
                   *[V.match_replace(sc2[:, h, :], m16[:, h, 0:8], sc[:, h, :], NEG) for h in range(2)])
                cl(*[V.max(m16[:, h, 8:16], sc2[:, h, :]) for h in range(2)])
                cl(*[V.max_index(i16[:, h, 8:16], m16[:, h, 8:16], sc2[:, h, :]) for h in range(2)])

            def topk_sums(cl, t):
                c2 = cand.rearrange("p (a b) -> p a b", a=TOPK)
                cl(tt(c2, m16[:, 0, :].rearrange("p (a b) -> p a b", b=1).broadcast_to([P, TOPK, TOPK]),
                      m16[:, 1, :].rearrange("p (a b) -> p a b", a=1).broadcast_to([P, TOPK, TOPK]), ALU.add))
                cl(V.max(top[:, 0:8], cand))
                cl(V.max_index(pos[:, 0:8], top[:, 0:8], cand), V.match_replace(cand2, top[:, 0:8], cand, NEG))
                cl(V.max(top[:, 8:16], cand2), ts(small[:, 0:1], top[:, 0:1], -1.0, None, ALU.mult))
                V.max_index(pos[:, 8:16], top[:, 8:16], cand2).then_inc(cand_ready, 1)
                dve.wait_ge(cand_ready, t + 1)

            def topk_experts(cl, t, par):
                cl(ts(ab[:, :, 0], pos[:, :], 4, None, ALU.logical_shift_right), ts(ab[:, :, 1], pos[:, :], 15, None, ALU.bitwise_and),
                   ts(i12[:, 0, :], i16[:, 0, :], float(NKEY), None, ALU.mult), V.tensor_copy(i12[:, 1, :], i16[:, 1, :]))
                e4 = eq.rearrange("p (k h j) -> p k h j", k=TOPK, h=2)
                cl(tt(e4, ab[:, :, :].rearrange("p k (h j) -> p k h j", j=1).broadcast_to([P, TOPK, 2, TOPK]),
                      iota[:, :].rearrange("p (k h j) -> p k h j", k=1, h=1).broadcast_to([P, TOPK, 2, TOPK]), ALU.is_equal))
                cl(tt(e4, e4, i12.rearrange("p (k h) j -> p k h j", k=1).broadcast_to([P, TOPK, 2, TOPK]), ALU.mult))
                cl(V.tensor_reduce(idf, eq.rearrange("p (k x) -> p k x", k=TOPK), AX.X, ALU.add))
                cl(V.tensor_copy(gidx[:, par, :], idf))
                dve.wait_ge(exp_done, t + 1)
                cl(V.reciprocal(small[:, 3:4], small[:, 1:2]))
                while cl.n < NT:
                    cl(ts(gate[:, par, :], e16, small[:, 3:4], None, ALU.mult))
                V.tensor_copy(small[:, 2:3], small[:, 3:4]).then_inc(topk_done, 1)

            def chain_of(t):
                return Chain(dve, topk_seq, t * NT, True)

            def dot(G, par, k):
                s = k % SLOTS
                dve.wait_ge(row_in[s], G * 32 + (k // SLOTS + 1) * 16)
                V.tensor_tensor_reduce(rows[:, s, 0:D], rows[:, s, 0:D], h2c, 1.0, 0.0, ALU.mult, ALU.add,
                                       hid[:, par, k:k + 1]).then_inc(dot_done, 1)

            def make_diag(G, par, k):
                dve.wait_ge(gelu_done, G * TOPK + (k + 1))
                dve.wait_ge(v_done, G * TOPK + (k + SLOTS - 3))
                ts(diag[:, k % 4, :], ident[:, :], gel[:, par, k:k + 1], gate[:, par, k:k + 1], ALU.mult, ALU.mult).then_inc(diag_ready, 1)

            cl = chain_of(0)
            topk_keys(cl, 0)
            topk_sums(cl, 0)
            topk_experts(cl, 0, 0)
            with nc.vector.Fori(0, NBLK) as b:
                dve.wait_ge(h2c_ready, b + 1)
                dve.nop(nofuse=True)
                with nc.vector.Fori(0, HEADS // 2) as hp:
                    for e in range(2):
                        G = b * HEADS + hp * 2 + e
                        t = G + 1
                        cl = chain_of(t)
                        for k in range(TOPK):
                            if k == 4:
                                topk_keys(cl, t)
                            if k == 5:
                                topk_sums(cl, t)
                            if k == 6:
                                topk_experts(cl, t, 1 - e)
                            dot(G, e, k)
                            if k:
                                make_diag(G, e, k - 1)
                        make_diag(G, e, TOPK - 1)
                fl = Chain(dve, fin_seq, b * 6)
                pk = peer.rearrange("p (k t) -> p k t", k=KD)
                xb = xt[:, :, bass.ds(b * P, P)]
                dve.wait_ge(pt_mm, b + 1)
                for h in range(2):
                    g2 = g2b[:, bass.ds(b, 1), 4 * h:4 * h + 4].rearrange("p a (k c) -> p (a k) c", c=1).broadcast_to([P, 4, P])
                    last = tt(pk[:, 4 * h:4 * h + 4, :], bank[4 + h][:, :].rearrange("p (k t) -> p k t", k=4), g2, ALU.mult)
                    fl(last)
                tt(xb, xb, pk, ALU.add).then_inc(x2_ready, 1)
                dve.wait_ge(frt, b + 1)
                fl(V.reciprocal(frs[:, :], frs[:, :]))
                fl(tt(pk, xb, frs[:, :].rearrange("p (a t) -> p a t", a=1).broadcast_to([P, KD, P]), ALU.mult))
                while fl.n < 6:
                    fl(V.tensor_copy(small[:, 2:3], eps_c[:, :]))
                nf = colv[:, COL_NF:COL_NF + KD].rearrange("p (k a) -> p k a", a=1).broadcast_to([P, KD, P])
                tt(pk, pk, nf, ALU.mult).then_inc(out_ready, 1)

        @block.gpsimd
        def _(pool):
            G_ = nc.gpsimd
            link = Chain(pool, pool_seq)
            link(G_.memset(ident[:, :], 0.0), G_.memset(ones[:, :], 1.0), G_.memset(zeros[:, :], 0.0),
                 G_.memset(headones[:, :], 0.0), G_.memset(eps_c[:, :], EPS))
            link(G_.affine_select(out=ident[:, :], in_=ident[:, :], compare_op=ALU.not_equal, fill=1.0, base=0,
                                  pattern=[[-1, P]], channel_multiplier=1))
            link(G_.memset(headones[0:64, 0:64], 1.0), G_.memset(headones[64:128, 64:128], 1.0))
            G_.iota(iota[:, :], [[1, TOPK]], base=0, channel_multiplier=0, allow_small_or_imprecise_dtypes=True).then_inc(consts, 1)
            pool.wait_ge(p9_ready, 1)
            pool.wait_ge(ld_ssm, 32)
            for q4 in range(0, NQ, 4):
                q = slice(q4, q4 + 4)
                w = P9 if q4 < NPAIR else P9r
                J = Q + 1
                pw = [w[:, :, r, q].rearrange("p s (q a) -> p q s a", a=1).broadcast_to([P, 4, J, GC]) for r in range(2)]
                cv = [bcs[:, 2 + r, q, :].rearrange("p q (a c) -> p q a c", a=1).broadcast_to([P, 4, J, GC]) for r in range(2)]
                o = [CP[:, r, q, :, :] for r in range(2)]
                T_ = G_.tensor_tensor
                link(T_(o[0], pw[0], cv[0], ALU.mult), T_(tp, pw[1], cv[1], ALU.mult))
                link(T_(o[0], o[0], tp, ALU.subtract))
                link(T_(o[1], pw[0], cv[1], ALU.mult), T_(tp, pw[1], cv[0], ALU.mult))
                link(T_(o[1], o[1], tp, ALU.add))
                link(G_.tensor_scalar(o[1], o[1], -1.0, None, ALU.mult))
            G_.memset(scan_a[:, :, :], 0.0).then_inc(cp_ready, 1)
            pool.wait_ge(s_ev, 16)
            pool.wait_ge(cp_ready, 1)
            link(G_.tensor_copy(fin[:, :, :], HHs[:, NCC, :, :]))
            link(G_.tensor_copy(HHs[:, NCC, :, :], ssmv[:, 3:5, :]), G_.memset(HHs[:, 0, :, :], 0.0))

            def step(cl, prev, cur):
                cl(G_.tensor_tensor(scan_a[:, :, :], prev, AR[:, :, :], ALU.mult),
                   G_.tensor_tensor(scan_b[:, 0, :], prev[:, 1, :], AI[:, 0, :], ALU.mult),
                   G_.tensor_tensor(scan_b[:, 1, :], prev[:, 0, :], AI[:, 1, :], ALU.mult))
                cl(G_.tensor_tensor(scan_a[:, :, :], scan_a[:, :, :], cur, ALU.add))
                cl(G_.tensor_tensor(cur, scan_a[:, :, :], scan_b[:, :, :], ALU.add))

            def at(slot):
                return HHs[:, bass.ds(slot, 1), :, :].rearrange("p a r x -> p (a r) x")

            base, STEP_OPS = link.n, 5
            for first, steps in ((0, NCC - 1), (NCC, NCL - 1)):
                with nc.gpsimd.Fori(0, steps // 3) as i:
                    cl = Chain(pool, pool_seq, i * (3 * STEP_OPS) + base, True)
                    for j in range(3):
                        step(cl, at(i * 3 + (first + j)), at(i * 3 + (first + j + 1)))
                base += steps * STEP_OPS
            link.n = base
            step(link, HHs[:, NCC - 1, :, :], fin[:, :, :])
            G_.memset(scan_a[:, :, :], 0.0).then_inc(scan_seq, 1)
            pool.sem_inc(v_done, SLOTS)
            with nc.gpsimd.Fori(0, NBLK * HEADS // 2) as g2:
                for e in range(2):
                    G = g2 * 2 + e
                    pool.wait_ge(topk_done, G + 1)
                    for k in range(TOPK):
                        pool.wait_ge(v_done, G * TOPK + (k + 1))
                        pool.nop(nofuse=True)
                        G_.indirect_dma_start(rows[:, k % SLOTS, :], None, table,
                                              bass.IndirectOffsetOnAxis(gidx[:, e, k:k + 1], 0)).then_inc(row_in[k % SLOTS], 16)
    return nc


def _layout(i):
    import numpy as np

    def colt(v):
        return np.asarray(v).reshape(-1, P).T

    a = {k: np.asarray(v) for k, v in i.items()}
    x = np.concatenate([a["x_prompt"][0], a["x_sample"][0]], axis=0)
    out = {"xT": x.reshape(T, KD, P).transpose(2, 1, 0)}
    out["condT"] = np.stack([a["c_ctx"], a["c"][0]]).reshape(2, KD, P).transpose(2, 1, 0)
    out["cols"] = np.concatenate(
        [colt(a["b_mod"][0]), colt(a["norm1_g"][0]), colt(a["norm2_g"][0]), colt(a["final_norm_g"]),
         colt(a["b_glu"][0]), colt(a["conv_w"][0]), colt(a["conv_b"][0]), colt(a["out_norm_g"][0])], axis=1)
    out["w_mod"] = a["w_mod"][0]
    w_in = a["w_in"][0]
    out["w_u"] = w_in[:, :DS].reshape(KD, P, DS).transpose(1, 0, 2)

    def tiles(w):
        return w.reshape(w.shape[0] // P, P, -1, P).transpose(2, 1, 0, 3)

    cb, cc, ch = (tiles(w_in[:, DS + j * DC:DS + (j + 1) * DC]) for j in range(3))
    conv = np.stack([cc, ch, cb], axis=1).reshape(3 * KS, P, KD, P)
    glu = tiles(a["w_glu"][0])
    glu = np.concatenate([glu, np.zeros_like(glu)], axis=2)
    out["w_tiles"] = np.concatenate([conv, glu, tiles(a["w_out"][0])], axis=0)

    def states(v):
        v = v.reshape((2, NPAIR, 2, NS) + v.shape[3:])
        v = np.moveaxis(v, (2, 3), (0, 1))
        return v.reshape((P, NQ) + v.shape[4:])

    dt = np.broadcast_to(a["log_dt"][0][:, :, None], (2, NG, NS))
    out["ssm"] = np.stack([states(v) for v in (a["lam_re"][0], a["lam_im"][0], dt, a["state_ssm_re"][0, 0], a["state_ssm_im"][0, 0])], axis=1)
    out["bc"] = np.stack([states(a["b_re"][0]), states(a["b_im"][0]),
                          states(a["c_re"][0].transpose(0, 1, 3, 2)), states(a["c_im"][0].transpose(0, 1, 3, 2))], axis=1)
    out["dskip"] = np.broadcast_to(a["d_skip"][0][None], (NCH, DS))
    out["skT"] = a["sub_keys"][0].transpose(2, 0, 1)
    out["w_query"] = a["w_query"][0].reshape(KD, P, -1).transpose(1, 0, 2)
    out["table"] = np.concatenate([a["expert_u"][0], a["expert_v"][0]], axis=1)
    return {k: np.ascontiguousarray(v) for k, v in out.items()}


def kernel(**inputs):
    import numpy as np
    import concourse.bacc as bacc
    from concourse.bass_utils import run_bass_kernel_spmd

    arrays = _layout(inputs)
    nc = bacc.Bacc("TRN2", target_bir_lowering=False, num_devices=1)
    args = [nc.dram_tensor(n, a.shape, mybir.dt.from_np(a.dtype), kind="ExternalInput").ap() for n, a in arrays.items()]
    args.append(nc.dram_tensor("y_out", (P, KD, T), F32, kind="ExternalOutput").ap())
    args.append(nc.dram_tensor("st_out", (P, 2, NQ), F32, kind="ExternalOutput").ap())
    args.append(nc.dram_tensor("kfull", (DS, NLAG * GC), F32, kind="Internal").ap())
    build(nc, *args)
    r = run_bass_kernel_spmd(nc, [arrays], core_ids=[0]).results[0]
    y = np.ascontiguousarray(r["y_out"].transpose(2, 1, 0)).reshape(T, D)
    st = r["st_out"].reshape(2, NS, 2, 2, NPAIR).transpose(2, 3, 4, 0, 1).reshape(2, 1, 1, 2, NG, NS)
    return (np.ascontiguousarray(y[:CTX]).reshape(1, CTX, D), np.ascontiguousarray(y[CTX:]).reshape(1, LAT, D),
            np.ascontiguousarray(st[0]), np.ascontiguousarray(st[1]))
```

```python
from contextlib import ExitStack

import concourse.bass as bass
from concourse import mybir

F32 = mybir.dt.float32
U32 = mybir.dt.uint32
I32 = mybir.dt.int32
ALU = mybir.AluOpType
ACT = mybir.ActivationFunctionType
AX = mybir.AxisListType

P = 128
D = 1024
KD = D // P
CTX = 128
LAT = 512
T = CTX + LAT
NBLK = T // P
ROW_W = 64
DS = D // 2
DC = D // 2
KS = DS // P
GC = 16
NG = DS // GC
NPAIR = NG // 2
NS = 64
Q = 8
NCC = CTX // Q
NCL = LAT // Q
NCH = NCC + NCL
NQ = 2 * NPAIR
NLAG = 2 * Q - 1
NMOD = 6
NMT = NMOD * KD
MCH = 2
HEADS = 8
TOPK = 16
NKEY = 128
DQ = 256
SLOTS = 8
EPS = 1e-6
NEG = -3.0e38
TWO_PI = 6.283185307179586
PI_IN = 3.1415925
C1 = 6.28125
C2 = 0.0019350051879882812
C3 = TWO_PI - C1 - C2

COL_BMOD = 0
COL_N1 = COL_BMOD + NMT
COL_N2 = COL_N1 + KD
COL_NF = COL_N2 + KD
COL_BGLU = COL_NF + KD
COL_CW = COL_BGLU + KS
COL_CB = COL_CW + 3 * KS
COL_OG = COL_CB + KS
NCOL = COL_OG + KD


class Chain:

    def __init__(self, eng, sem, base=0):
        self.eng, self.sem, self.n, self.base = eng, sem, 0, base

    def __call__(self, *instructions, hold=False):
        for ins in instructions:
            self.n += 1
            ins.then_inc(self.sem, 1)
        self.eng.wait_ge(self.sem, self.n + self.base)
        if hold:
            self.eng.nop(nofuse=True)


def build(nc, xT, condT, cols, w_mod, w_u, w_tiles, w_o, ssm, bc, dskip, skT, w_query, table, y_out, st_out, kfull):
    ctx = ExitStack()
    with ctx:
        def sb(name, shape, dt=F32):
            return ctx.enter_context(nc.sbuf_tensor(name, shape, dt))

        def sem(name):
            return ctx.enter_context(nc.semaphore(name))

        bank = [ctx.enter_context(nc.psum_tensor(f"bank{i}", [P, 512], F32)) for i in range(8)]

        hT_r = sb("hT_r", [P, KD * T])
        x_r = sb("x_r", [P, KD * T])
        mix_r = sb("mix_r", [P, KD * T])
        r1 = sb("r1", [P, 17408])
        r2 = sb("r2", [P, 17408])

        hT = hT_r[:, :].rearrange("p (k t) -> p k t", k=KD)
        Y = hT_r[0:NCH, 0:Q * DS].rearrange("p (t c) -> p t c", t=Q)
        xt = x_r[:, :].rearrange("p (k t) -> p k t", k=KD)
        uc = x_r[0:NCH, 0:Q * DS].rearrange("p (g s c) -> p g s c", g=NG, s=Q)
        dsk = x_r[0:NCH, Q * DS:Q * DS + DS]
        BP = [r[:, 0:4096].rearrange("p (r q s c) -> p r q s c", r=2, q=NPAIR, s=Q) for r in (x_r, mix_r)]
        mix = mix_r[:, :].rearrange("p (k t) -> p k t", k=KD)
        Ksb = mix_r[0:2 * GC, 0:NPAIR * NLAG * GC].rearrange("p (q x) -> p q x", q=NPAIR)
        Bb = mix_r[:, 4096:5120].rearrange("p (r q c) -> p r q c", r=2, q=NQ)
        cc_t = mix_r[:, 0:T]
        pr_t = mix_r[:, T:2 * T]
        cv_t = mix_r[:, 2 * T:3 * T]
        BPT = r1[:, 0:8192].rearrange("p (q r n) -> p q r n", q=NQ, r=2)
        CP = r1[:, 8192:17408].rearrange("p (r q j c) -> p r q j c", r=2, q=NQ, j=Q + 1)
        M = r1[:, 0:4096].rearrange("p (g x) -> p g x", g=NG)
        Hb = r1[:, 4096:4096 + NCH * 2 * NPAIR].rearrange("p (c r q) -> p c r q", c=NCH, r=2)
        wm = r2[:, 0:4096].rearrange("p (a k m) -> p a k m", a=2, k=KD)
        gT = r2[:, 0:KS * T].rearrange("p (k t) -> p k t", k=KS)
        wu = r2[:, 4096:8192].rearrange("p (k m) -> p k m", k=KD)
        Bd = r2[:, 0:2048].rearrange("p (r q c) -> p r q c", r=2, q=NQ)
        U = r2[:, 4096:4096 + NG * NCH].rearrange("p (g c) -> p g c", g=NG)
        HH = r2[:, 8192:8192 + NCH * 64].rearrange("p (c r d q) -> p c r d q", c=NCH, r=2, d=2)
        HHs = r2[:, 8192:8192 + NCH * 64].rearrange("p (c r x) -> p c r x", c=NCH, r=2)
        bcs = r2[:, 8192:8192 + 2048].rearrange("p (v q c) -> p v q c", v=4, q=NQ)
        P9 = r2[:, 10240:10816].rearrange("p (j r q) -> p j r q", j=Q + 1, r=2)
        P9r = r2[:, 10816:11392].rearrange("p (j r q) -> p j r q", j=Q + 1, r=2)
        tp = r2[:, 11392:11968].rearrange("p (q j c) -> p q j c", q=4, j=Q + 1)
        tv = r2[:, 11968:12992].rearrange("p (q s c) -> p q s c", q=8, s=Q)
        wt = r2[:, 13312:15360].rearrange("p (a k m) -> p a k m", a=2, k=KD)
        wo = r1[:, 0:8192].rearrange("p (m k c) -> p m k c", m=KD, k=KD)
        rs = r2[:, 15360:15360 + T]
        rs2 = r1[:, 16384:16384 + T]
        sq = [r2[:, 16000:16000 + T], r2[:, 16640:16640 + T]]
        sq2 = [r1[:, 8192:8192 + T], r1[:, 8192 + T:8192 + 2 * T]]
        rows = r1[:, 0:SLOTS * 2 * D].rearrange("p (s x) -> p s x", s=SLOTS)
        wq = r2[:, 0:KD * 2048].rearrange("p (k m) -> p k m", k=KD)
        peer = r2[:, 16384:17408]

        def mx(a, n):
            return mix_r[:, a:a + n]
        h2Tc = mx(0, 1024).rearrange("p (k t) -> p k t", k=KD)
        h2c = mx(1024, 1024)
        q_s = mx(2048, 256)
        qT = mx(2304, 256).rearrange("p (h t) -> p h t", h=2)
        sc = mx(2560, 256).rearrange("p (h n) -> p h n", h=2)
        sc2 = mx(2816, 256).rearrange("p (h n) -> p h n", h=2)
        cand = mx(3072, 256)
        cand2 = mx(3328, 256)
        eq = mx(3584, 512)
        diag = mx(4096, 512).rearrange("p (a m) -> p a m", a=4)
        m16 = mx(4608, 32).rearrange("p (h n) -> p h n", h=2)
        i12 = mx(4640, 32).rearrange("p (h n) -> p h n", h=2)
        e16 = mx(4672, 16)
        top = mx(4688, 16)
        hid = mx(4704, 32).rearrange("p (a n) -> p a n", a=2)
        gel = mx(4736, 32).rearrange("p (a n) -> p a n", a=2)
        gate = mx(4768, 32).rearrange("p (a n) -> p a n", a=2)
        g2b = mx(4800, NBLK * KD).rearrange("p (b k) -> p b k", b=NBLK)

        idf = mx(4848, TOPK)

        ident = sb("ident", [P, P])
        ones = sb("ones", [P, P])
        zeros = sb("zeros", [P, P])
        headones = sb("headones", [P, P])
        iota = sb("iota", [P, TOPK])
        colv = sb("colv", [P, NCOL])
        cond = sb("cond", [P, KD, 2])
        modT = sb("modT", [P, NMT, 2])
        modrow = sb("modrow", [2, 2, MCH * P])
        gs = sb("gs", [P, KD, 2])
        ssmv = sb("ssmv", [P, 5, NQ])
        sv = sb("sv", [P, 12, NQ])
        kint = sb("kint", [P, NQ], I32)
        AR = sb("AR", [P, 2, NQ])
        AI = sb("AI", [P, 2, NQ])
        fin = sb("fin", [P, 2, NQ])
        scan_a = sb("scan_a", [P, 2, NQ])
        scan_b = sb("scan_b", [P, 2, NQ])
        sk = sb("sk", [P, 2, NKEY])
        eps_c = sb("eps_c", [P, 1])
        frs = sb("frs", [P, P])
        small = sb("small", [P, 4])
        i16 = sb("i16", [P, 2, TOPK], U32)
        pos = sb("pos", [P, TOPK], U32)
        ab = sb("ab", [P, TOPK, 2], U32)
        gidx = sb("gidx", [P, 2, TOPK], U32)

        def col(a, n=1):
            return colv[:, a:a + n]

        ld_cond = sem("ld_cond")
        ld_ssm = sem("ld_ssm")
        ld_x = sem("ld_x")
        ld_x2 = sem("ld_x2")
        ld_wu = sem("ld_wu")
        ld_sk = sem("ld_sk")
        ld_dsk = sem("ld_dsk")
        ld_wq = sem("ld_wq")
        ld_m = sem("ld_m")
        ld_wo = sem("ld_wo")
        wm_in = [sem(f"wm_in{i}") for i in range(2)]
        wt_in = [sem(f"wt_in{i}") for i in range(2)]
        row_in = [sem(f"row_in{i}") for i in range(SLOTS)]
        consts = sem("consts")
        silu_done = sem("silu_done")
        mod_mm = sem("mod_mm")
        mod_row = sem("mod_row")
        mod_tr = sem("mod_tr")
        mod_free = sem("mod_free")
        mod_ready = sem("mod_ready")
        bp_ready = sem("bp_ready")
        bpt_mm = sem("bpt_mm")
        bpt_ev = sem("bpt_ev")
        cp_ready = sem("cp_ready")
        p9_ready = sem("p9_ready")
        bb_ready = sem("bb_ready")
        ssm_act = sem("ssm_act")
        ssm_dve = sem("ssm_dve")
        k_mm = sem("k_mm")
        k_ev = sem("k_ev")
        k_out = sem("k_out")
        sq_ready = sem("sq_ready")
        sq_used = sem("sq_used")
        rms_act = sem("rms_act")
        xs_ready = sem("xs_ready")
        h_ready = sem("h_ready")
        u_mm = sem("u_mm")
        u_ev = sem("u_ev")
        ut_mm = sem("ut_mm")
        ut_ev = sem("ut_ev")
        ud_ready = sem("ud_ready")
        s_mm = sem("s_mm")
        s_ev = sem("s_ev")
        scan_seq = sem("scan_seq")
        hb_ready = sem("hb_ready")
        z_mm = sem("z_mm")
        cc_ev = sem("cc_ev")
        ch_ev = sem("ch_ev")
        cb_ev = sem("cb_ev")
        conv_seq = sem("conv_seq")
        dve_seq = sem("dve_seq")
        act_seq = sem("act_seq")
        pool_seq = sem("pool_seq")
        y_mm = sem("y_mm")
        y_ev = sem("y_ev")
        y_gelu = sem("y_gelu")
        gt_mm = sem("gt_mm")
        gt_ev = sem("gt_ev")
        glu_sig = sem("glu_sig")
        glu_ev = sem("glu_ev")
        mix_ready = sem("mix_ready")
        x1_ready = sem("x1_ready")
        h2_staged = sem("h2_staged")
        q_mm = sem("q_mm")
        q_ev = sem("q_ev")
        qt_mm = sem("qt_mm")
        qt_ev = sem("qt_ev")
        sc_mm = sem("sc_mm")
        sc_ev = sem("sc_ev")
        cand_ready = sem("cand_ready")
        exp_done = sem("exp_done")
        topk_done = sem("topk_done")
        topk_seq = sem("topk_seq")
        h2c_mm = sem("h2c_mm")
        h2c_ready = sem("h2c_ready")
        dot_done = sem("dot_done")
        gelu_done = sem("gelu_done")
        diag_ready = sem("diag_ready")
        v_done = sem("v_done")
        peer_ev = sem("peer_ev")
        pt_mm = sem("pt_mm")
        x2_ready = sem("x2_ready")
        fsq_ready = sem("fsq_ready")
        fs_mm = sem("fs_mm")
        frt = sem("frt")
        out_ready = sem("out_ready")
        out_dma = sem("out_dma")
        fin_seq = sem("fin_seq")
        st_dma = sem("st_dma")

        NM1 = 2 * KD // MCH
        NM2 = NMT // MCH - NM1
        NM_BODY = NM2 // KS
        assert NM2 % KS == 0 and NM_BODY == 4
        MOD_AT = [(), (0, 1), (2, 3)]
        MOD_LOAD_AT = [(0, 1), (2, 3), ()]
        NCONV = 3 * KS
        SQ_CONV, SQ_SSM, SQ_2 = KD, KD + KS, KD + 2 * KS
        RT_CONV, RT_SSM, RT_2 = 1, 1 + KS, 2 + KS
        XS_CONV, XS_SSM, XS_2 = KD, KD + KS, KD + KS + 1

        block = ctx.enter_context(nc.Block())

        NORM_AT = [1, 3, 5, 6]
        TOPK_AT = 4
        EXP_AT = TOPK_AT + 3

        @block.sync
        def _(sp):
            w_mod_v = w_mod.rearrange("(k p) m -> p k m", p=P)
            CW = MCH * P
            sp.dma_start(cond[:, :, :], condT).then_inc(ld_cond, 16)
            sp.dma_start(colv[:, :], cols).then_inc(ld_cond, 16)
            sp.dma_start(ssmv[:, :, :], ssm).then_inc(ld_ssm, 16)
            sp.dma_start(bcs, bc).then_inc(ld_ssm, 16)
            for n in range(2):
                sp.dma_start(wm[:, n, :, :], w_mod_v[:, :, n * CW:(n + 1) * CW]).then_inc(wm_in[n], 16)
            sp.dma_start(hT, xT).then_inc(ld_x, 16)
            with nc.sync.Fori(1, NM1 // 2) as i:
                for a in range(2):
                    sp.wait_ge(mod_mm, i * 2 + a - 1)
                    sp.dma_start(wm[:, a, :, :], w_mod_v[:, :, bass.ds((i * 2 + a) * CW, CW)]).then_inc(wm_in[a], 16)
            sp.dma_start(wu, w_u).then_inc(ld_wu, 16)
            sp.dma_start(sk[:, :, :], skT).then_inc(ld_sk, 16)
            for n in range(2):
                sp.dma_start(wt[:, n, :, :], w_tiles[n]).then_inc(wt_in[n], 16)
            sp.wait_ge(bpt_mm, 16)
            sp.dma_start(dsk, dskip).then_inc(ld_dsk, 16)
            sp.wait_ge(k_ev, 8)
            sp.dma_start(kfull.rearrange("(q p) x -> p q x", p=2 * GC), Ksb).then_inc(k_out, 16)

            def mod_load(i, j):
                sp.wait_ge(mod_mm, i * NM_BODY + (NM1 + j - 1))
                sp.dma_start(wm[:, j % 2, :, :],
                             w_mod_v[:, :, bass.ds((i * NM_BODY + (NM1 + j)) * CW, CW)]).then_inc(wm_in[j % 2], 16)

            with nc.sync.Fori(0, KS // 2) as i2:
                for e in range(2):
                    i = i2 * 2 + e
                    for r in range(3):
                        for j in MOD_LOAD_AT[r]:
                            mod_load(i, j)
                        n = 3 * e + r
                        sp.wait_ge(z_mm, i * 3 + r + 1)
                        sp.dma_start(wt[:, n % 2, :, :],
                                     w_tiles[bass.ds(i * 3 + (r + 2), 1)].rearrange("a p k m -> p (a k) m")
                                     ).then_inc(wt_in[n % 2], 16)
            sp.wait_ge(y_mm, NG // 4)
            for h in range(2):
                m = slice(4 * h, 4 * h + 4)
                sp.dma_start(wo[:, m, :, :], w_o[:, m, :, :]).then_inc(ld_wo, 16)
            sp.wait_ge(y_ev, NG // 4)
            sp.dma_start(xt, xT).then_inc(ld_x2, 16)
            sp.dma_start(st_out, fin[:, :, :]).then_inc(st_dma, 16)
            for k in range(2, 6):
                sp.dma_start(wq[:, k, :], w_query[:, k, :]).then_inc(ld_wq, 16)
            sp.wait_ge(z_mm, NCONV + KS)
            sp.wait_ge(mix_ready, KS)
            for k in (6, 7):
                sp.dma_start(wq[:, k, :], w_query[:, k, :]).then_inc(ld_wq, 16)
            sp.wait_ge(glu_ev, KS)
            for k in (0, 1):
                sp.dma_start(wq[:, k, :], w_query[:, k, :]).then_inc(ld_wq, 16)
            with nc.sync.Fori(0, NBLK) as b:
                sp.wait_ge(out_ready, b + 1)
                sp.dma_start(y_out[:, :, bass.ds(b * P, P)], peer.rearrange("p (k t) -> p k t", k=KD)).then_inc(out_dma, 16)
            sp.wait_ge(out_dma, 16 * NBLK + 16)
            sp.wait_ge(st_dma, 16)
            sp.wait_ge(k_out, 16)

        @block.tensor
        def _(pe):
            mm = nc.tensor.matmul

            def mod_step(turn, chunk, a):
                pe.wait_ge(wm_in[a], turn * 16 + 16)
                pe.wait_ge(mod_free, chunk + 1)
                for k in range(KD):
                    last = mm(bank[6 + a][0:2, 0:MCH * P], cond[:, k, :], wm[:, a, k, :], start=(k == 0), stop=(k == KD - 1))
                last.then_inc(mod_mm, 1)

            def mod_turn(chunk, a):
                pe.wait_ge(mod_row, chunk + 1)
                for m in range(MCH):
                    last = mm(bank[6 + a][:, MCH * P + 2 * m:MCH * P + 2 * m + 2], modrow[:, a, m * P:(m + 1) * P],
                              ident[0:2, 0:2], start=True, stop=True)
                last.then_inc(mod_tr, 1)

            pe.wait_ge(consts, 1)
            pe.wait_ge(silu_done, 1)
            with nc.tensor.Fori(0, NM1 // 4) as i:
                for a in range(2):
                    mod_step(i, i * 2 + a, a)
                for a in range(2):
                    mod_turn(i * 2 + a, a)

            def add_squares(first, k, count, w, s, b0, b1):
                pe.wait_ge(sq_ready, first + k + 1)
                mm(bank[b0][:, :], w[:, :], s[(first + k) % 2][:, CTX:T], start=(k == 0), stop=(k == count - 1))
                mm(bank[b1][:, 0:CTX], w[:, :], s[(first + k) % 2][:, 0:CTX], start=(k == 0), stop=(k == count - 1)).then_inc(sq_used, 1)

            def turn_input(g):
                if g % 8 == 0:
                    pe.wait_ge(bp_ready, g // 8 + 1)
                q0 = (g % 8) * 2
                if g >= 2:
                    pe.wait_ge(bpt_ev, g - 1)
                for j in range(4):
                    src = BP[g // 8][:, j % 2, q0 + j // 2, :, :].rearrange("p s c -> p (s c)")
                    last = nc.tensor.transpose(bank[g % 2][:, j * P:(j + 1) * P], src, ident[:, :])
                last.then_inc(bpt_mm, 1)

            for k in range(KD):
                add_squares(0, k, KD, ones, sq, 4, 5)
            for g in range(8):
                turn_input(g)
            with nc.tensor.Fori(NM1 // 4, NM1 // 2) as i:
                for a in range(2):
                    mod_step(i, i * 2 + a, a)
                for a in range(2):
                    mod_turn(i * 2 + a, a)

            pe.wait_ge(ld_wu, 16)
            for s in range(0, Q, 2):
                if s == 2:
                    pe.wait_ge(bpt_ev, 16)
                if s >= 4:
                    pe.wait_ge(u_ev, s - 2)
                for k in range(KD):
                    if s == 0:
                        turn_input(8 + k)
                        pe.wait_ge(h_ready, k + 1)
                    for e in range(2):
                        last = mm(bank[(s + e + 2) % 4][0:NCH, :], hT[:, k, s + e:T:Q], wu[:, k, :], start=(k == 0), stop=(k == KD - 1))
                        if k == KD - 1:
                            last.then_inc(u_mm, 1)
            pe.wait_ge(u_ev, Q)
            for g4 in range(NG // 4):
                if g4 >= 2:
                    pe.wait_ge(ut_ev, g4 - 1)
                for j in range(4):
                    g = 4 * g4 + j
                    last = nc.tensor.transpose(bank[2 + g4 % 2][:, j * NCH:(j + 1) * NCH], uc[:, g, :, :].rearrange("p s c -> p (s c)"), ident[0:NCH, 0:NCH])
                last.then_inc(ut_mm, 1)
            pe.wait_ge(ut_ev, NG // 4)
            pe.wait_ge(bpt_ev, 16)
            for g in range(16):
                if g >= 2:
                    pe.wait_ge(s_ev, g - 1)
                for j in range(2):
                    q = 2 * g + j
                    for r in range(2):
                        for a in range(2):
                            last = mm(bank[4 + g % 2][64 * a:64 * a + 64, (2 * j + r) * NCH:(2 * j + r + 1) * NCH],
                                      BPT[:, q, r, 64 * a:64 * a + 64], U[:, 2 * (q % NPAIR) + a, :], start=True, stop=True)
                last.then_inc(s_mm, 1)

            pe.wait_ge(bb_ready, 2)
            pe.wait_ge(cp_ready, 1)
            for g in range(8):
                d = g // 4
                if g >= 2:
                    pe.wait_ge(k_ev, g - 1)
                for j in range(4):
                    q = d * NPAIR + (g % 4) * 4 + j
                    for r in range(2):
                        last = mm(bank[2 + g % 2][0:2 * GC, j * P:(j + 1) * P], Bd[:, r, q, :],
                                  CP[:, r, q, d:d + Q, :].rearrange("p j c -> p (j c)"), start=(r == 0), stop=(r == 1))
                last.then_inc(k_mm, 1)

            def tile(w, kt, src, b0, b1):
                for k in range(kt):
                    mm(bank[b0][:, :], w[:, k, :], src[:, k, CTX:T], start=(k == 0), stop=(k == kt - 1))
                for k in range(kt):
                    last = mm(bank[b1][:, 0:CTX], w[:, k, :], src[:, k, 0:CTX], start=(k == 0), stop=(k == kt - 1))
                last.then_inc(z_mm, 1)

            pe.wait_ge(k_ev, 8)
            pe.wait_ge(s_ev, 16)
            with nc.tensor.Fori(0, KS // 2) as i2:
                for e in range(2):
                    i = i2 * 2 + e
                    for r in range(3):
                        for j in MOD_AT[r]:
                            mod_step(i * (NM_BODY // 2) + (NM1 // 2 + j // 2), i * NM_BODY + (NM1 + j), j % 2)
                        pe.wait_ge((cc_ev, ch_ev, cb_ev)[r], i + 1)
                        n = 3 * e + r
                        pe.wait_ge(wt_in[n % 2], i2 * 48 + (n // 2 + 1) * 16)
                        tile(wt[:, n % 2, :, :], KD, hT, r, 3 + r)
                        for j in MOD_AT[r]:
                            mod_turn(i * NM_BODY + (NM1 + j), j % 2)

            pe.wait_ge(ld_m, 16 * Q)
            pe.wait_ge(hb_ready, 2)
            pe.wait_ge(cc_ev, KS + 1)
            pe.wait_ge(ch_ev, KS + 1)
            pe.wait_ge(mod_free, NMT // MCH + 2)
            for g4 in range(NG // 4):
                if g4 >= 2:
                    pe.wait_ge(y_ev, g4 - 1)
                a = g4 % 2
                for j in range(4):
                    pr = 4 * (g4 // 2) + j
                    g = 2 * pr + a
                    out = bank[g4 % 2][0:NCH, j * P:(j + 1) * P]
                    mm(out, U[:, g, :], M[:, g, :], start=True, stop=False)
                    rows_a = slice(64 * a, 64 * a + 64)
                    for r in range(2):
                        mm(out, HH[rows_a, :, r, 0, pr], CP[rows_a, r, pr, 1:Q + 1, :].rearrange("p j c -> p (j c)"),
                           start=False, stop=False)
                        last = mm(out, Hb[rows_a, :, r, pr], CP[rows_a, r, NPAIR + pr, 0:Q, :].rearrange("p j c -> p (j c)"),
                                  start=False, stop=(r == 1))
                last.then_inc(y_mm, 1)
                if g4 in NORM_AT:
                    m = NORM_AT.index(g4)
                    if m >= 1:
                        pe.wait_ge(rms_act, 2 * (RT_CONV + m))
                    add_squares(SQ_CONV + m, 0, 1, headones, sq, 6, 7)
            pe.wait_ge(cb_ev, KS + 1)
            for n in range(2 * KS):
                cb_, th = n // 2, n % 2
                pe.wait_ge(y_gelu, cb_ + 1)
                if n >= 2:
                    pe.wait_ge(gt_ev, n - 1)
                for j in range(4):
                    last = nc.tensor.transpose(bank[2 + n % 2][:, j * NCH:(j + 1) * NCH],
                                               Y[:, 4 * th + j, cb_ * P:(cb_ + 1) * P], ident[0:NCH, 0:NCH])
                last.then_inc(gt_mm, 1)
            pe.wait_ge(gt_ev, 2 * KS)
            for m in range(KS):
                if m >= 2:
                    pe.wait_ge(glu_sig, 2 * (m - 1))
                pe.wait_ge(wt_in[m // 2], (NCONV // 2 + 1) * 16)
                tile(wt[:, m // 2, (m % 2) * KS:(m % 2 + 1) * KS, :], KS, gT, m % 2, 2 + m % 2)
            for m in range(KS):
                add_squares(SQ_SSM, m, KS, ones, sq2, 4, 5)
            def out_part(m, first, ks):
                for k in ks:
                    mm(bank[m % 2][:, :], wo[:, m, k, :], mix[:, k, CTX:T], start=first and k == ks[0], stop=not first and k == ks[-1])
                for k in ks:
                    last = mm(bank[2 + m % 2][:, 0:CTX], wo[:, m, k, :], mix[:, k, 0:CTX],
                              start=first and k == ks[0], stop=not first and k == ks[-1])
                return last

            conv_half, ssm_half = range(KS, KD), range(KS)
            pe.wait_ge(ld_wo, 32)
            pe.wait_ge(mix_ready, KS)
            pe.wait_ge(glu_sig, 2 * KS)
            out_part(0, True, conv_half)
            out_part(1, True, conv_half)
            pe.wait_ge(mix_ready, KD)
            for m in range(KD):
                if m >= 2:
                    pe.wait_ge(x1_ready, 2 * (m - 1))
                    out_part(m, True, conv_half)
                out_part(m, False, ssm_half).then_inc(z_mm, 1)
                if m >= 1:
                    add_squares(SQ_2, m - 1, KD, ones, sq2, 4, 5)
            add_squares(SQ_2, KD - 1, KD, ones, sq2, 4, 5)

            def query(t, col0):
                pe.wait_ge(h2_staged, t + 1)
                for k in range(KD):
                    last = mm(bank[2][:, 0:DQ], h2Tc[:, k, :], wq[:, k, bass.ds(col0, DQ)], start=(k == 0), stop=(k == KD - 1))
                last.then_inc(q_mm, 1)

            def query_turn(t):
                pe.wait_ge(q_ev, t + 1)
                for h in range(2):
                    last = nc.tensor.transpose(bank[3][:, h * P:(h + 1) * P], q_s[:, h * P:(h + 1) * P], ident[:, :])
                last.then_inc(qt_mm, 1)

            def scores(t):
                pe.wait_ge(qt_ev, t + 1)
                for h in range(2):
                    last = mm(bank[6][:, h * P:(h + 1) * P], qT[:, h, :], sk[:, h, :], start=True, stop=True)
                last.then_inc(sc_mm, 1)

            def add_rows(n, k):
                pe.wait_ge(diag_ready, n + k + 1)
                for h in range(2):
                    last = mm(bank[h][:, :], diag[:, k % 4, :], rows[:, k % SLOTS, D + h * 512:D + (h + 1) * 512],
                              start=False, stop=False, skip_group_check=True)
                last.then_inc(v_done, 1)

            pe.wait_ge(ld_wq, 16 * KD)
            pe.wait_ge(ld_sk, 16)
            pe.wait_ge(x1_ready, 2 * KD)
            for k in range(KD):
                pe.wait_ge(h_ready, KD + k + 1)
                last = mm(bank[2][:, 0:DQ], hT[:, k, 0:P], wq[:, k, 0:DQ], start=(k == 0), stop=(k == KD - 1))
            last.then_inc(q_mm, 1)
            query_turn(0)
            scores(0)
            with nc.tensor.Fori(0, NBLK) as b:
                pe.wait_ge(h2_staged, b * HEADS + 1)
                for k in range(KD):
                    last = nc.tensor.transpose(bank[4 + k // 4][:, (k % 4) * P:(k % 4 + 1) * P], h2Tc[:, k, :], ident[:, :])
                last.then_inc(h2c_mm, 1)
                pe.wait_ge(peer_ev, b + 1)
                for h in range(2):
                    for j in range(4):
                        mm(bank[h][:, j * P:(j + 1) * P], zeros[:, :], zeros[:, :], start=(j == 0), stop=False, skip_group_check=True)
                with nc.tensor.Fori(0, HEADS // 2) as hp:
                    for e in range(2):
                        G = b * HEADS + hp * 2 + e
                        t = G + 1
                        query(t, (t % HEADS) * DQ)
                        add_rows(G * TOPK, 0)
                        query_turn(t)
                        add_rows(G * TOPK, 1)
                        scores(t)
                        for k in range(2, TOPK):
                            add_rows(G * TOPK, k)
                pe.wait_ge(peer_ev, b + 2)
                for k in range(KD):
                    last = nc.tensor.transpose(bank[4 + k // 4][:, (k % 4) * P:(k % 4 + 1) * P], peer[:, k * P:(k + 1) * P], ident[:, :])
                last.then_inc(pt_mm, 1)
                pe.wait_ge(fsq_ready, b + 1)
                for k in range(KD):
                    last = mm(bank[7][:, 0:P], ones[:, :], peer[:, k * P:(k + 1) * P], start=(k == 0), stop=(k == KD - 1))
                last.then_inc(fs_mm, 1)

        @block.scalar
        def _(act):
            A = nc.scalar.activation
            link = Chain(act, act_seq)
            act.wait_ge(ld_cond, 32)
            A(cond[:, :, :], cond[:, :, :], ACT.Silu).then_inc(silu_done, 1)
            act.wait_ge(ld_ssm, 32)
            A(sv[:, 0, :], ssmv[:, 2, :], ACT.Exp).then_inc(ssm_act, 1)
            act.wait_ge(ssm_dve, 1)
            A(sv[:, 3, :], sv[:, 1, :], ACT.Exp).then_inc(ssm_act, 1)
            act.wait_ge(ssm_dve, 2)
            A(sv[:, 6, :], sv[:, 4, :], ACT.Sin).then_inc(ssm_act, 1)
            A(sv[:, 7, :], sv[:, 5, :], ACT.Sin).then_inc(ssm_act, 1)

            act.sem_inc(mod_free, 2)
            act.sem_inc(cc_ev, 1)
            act.sem_inc(ch_ev, 1)
            act.sem_inc(cb_ev, 1)
            act.sem_inc(peer_ev, 1)
            act.sem_inc(out_dma, 16)

            def mod_rows(chunk, a):
                act.wait_ge(mod_mm, chunk + 1)
                A(modrow[:, a, :], bank[6 + a][0:2, 0:MCH * P], ACT.Copy).then_inc(mod_row, 1)

            def mod_take(chunk, a):
                act.wait_ge(mod_tr, chunk + 1)
                for m in range(MCH):
                    at = chunk * MCH + m
                    last = A(modT[:, bass.ds(at, 1), :].rearrange("p a c -> p (a c)"), bank[6 + a][:, MCH * P + 2 * m:MCH * P + 2 * m + 2],
                             ACT.Identity, bias=colv[:, bass.ds(at + COL_BMOD, 1)])
                last.then_inc(mod_free, 1)

            with nc.scalar.Fori(0, NM1 // 4) as i:
                for a in range(2):
                    mod_rows(i * 2 + a, a)
                for a in range(2):
                    mod_take(i * 2 + a, a)

            def take_input(g):
                act.wait_ge(bpt_mm, g + 1)
                A(BPT[:, 2 * g:2 * g + 2, :, :].rearrange("p q r n -> p (q r n)"), bank[g % 2][:, :], ACT.Copy).then_inc(bpt_ev, 1)

            def square(src, place, s):
                if place >= 2:
                    act.wait_ge(sq_used, place - 1)
                A(s[place % 2], src, ACT.Square).then_inc(sq_ready, 1)

            def roots(used, o, b0, b1, width, xs):
                act.wait_ge(sq_used, used)
                if xs:
                    act.wait_ge(xs_ready, xs)
                A(o[:, 0:CTX], bank[b1][:, 0:CTX], ACT.Sqrt, scale=1.0 / width, bias=eps_c[:, 0:1]).then_inc(rms_act, 1)
                A(o[:, CTX:T], bank[b0][:, :], ACT.Sqrt, scale=1.0 / width, bias=eps_c[:, 0:1]).then_inc(rms_act, 1)

            def modulate(shift, k, c, lo, hi):
                return A(hT[:, k, lo:hi], hT[:, k, lo:hi], ACT.Identity, scale=gs[:, k, c:c + 1],
                         bias=modT[:, shift * KD + k, c:c + 1])

            act.wait_ge(consts, 1)
            act.wait_ge(ld_x, 16)
            for k in range(KD):
                square(hT[:, k, :], k, sq)
            roots(KD, rs, 4, 5, D, 0)
            for g in range(8):
                take_input(g)
            with nc.scalar.Fori(NM1 // 4, NM1 // 2) as i:
                for a in range(2):
                    mod_rows(i * 2 + a, a)
                for a in range(2):
                    mod_take(i * 2 + a, a)
            act.wait_ge(mod_ready, 1)
            for k in range(KD):
                act.wait_ge(xs_ready, k + 1)
                modulate(0, k, 0, 0, CTX)
                modulate(0, k, 1, CTX, T).then_inc(h_ready, 1)
                take_input(8 + k)
            for s in range(Q):
                act.wait_ge(u_mm, s + 1)
                A(uc[:, :, s, :], bank[(s + 2) % 4][0:NCH, :].rearrange("p (g c) -> p g c", g=NG), ACT.Copy).then_inc(u_ev, 1)
            for g4 in range(NG // 4):
                act.wait_ge(ut_mm, g4 + 1)
                A(U[:, 4 * g4:4 * g4 + 4, :].rearrange("p g c -> p (g c)"), bank[2 + g4 % 2][:, 0:4 * NCH], ACT.Copy).then_inc(ut_ev, 1)
            act.wait_ge(cp_ready, 1)
            act.wait_ge(bp_ready, 2)
            for g in range(16):
                d, pr = g // 8, (g % 8) * 2
                act.wait_ge(s_mm, g + 1)
                for r in range(2):
                    src = bank[4 + g % 2][:, 0:4 * NCH].rearrange("p (q r c) -> p c r q", q=2, r=2)[:, :, r, :]
                    if d == 0:
                        last = A(HH[:, 1:NCH, r, 0, pr:pr + 2], src[:, 0:NCH - 1, :], ACT.Copy)
                    else:
                        A(HH[:, NCC:0:-1, r, 1, pr:pr + 2], src[:, 0:NCC, :], ACT.Copy)
                        last = A(HH[:, NCH - 1:NCC:-1, r, 1, pr:pr + 2], src[:, NCC + 1:NCH, :], ACT.Copy)
                last.then_inc(s_ev, 1)
            act.wait_ge(k_out, 16)
            act.wait_ge(s_mm, 16)
            kv = kfull.rearrange("(g p) x -> p g x", p=GC)
            for s in range(Q):
                lag0 = (Q - 1 - s) * GC
                nc.scalar.dma_start(M[s * GC:(s + 1) * GC, :, :], kv[:, :, lag0:lag0 + P]).then_inc(ld_m, 16)
            with nc.scalar.Fori(0, KS) as i:
                act.wait_ge(z_mm, i * 3 + 1)
                act.wait_ge(ch_ev, i + 1)
                A(cc_t[:, CTX:T], bank[0][:, :], ACT.Copy)
                A(cc_t[:, 0:CTX], bank[3][:, 0:CTX], ACT.Copy).then_inc(cc_ev, 1)
                for r in range(3):
                    for j in MOD_AT[r]:
                        mod_rows(i * NM_BODY + (NM1 + j), j % 2)
                    for j in MOD_AT[r]:
                        mod_take(i * NM_BODY + (NM1 + j), j % 2)
            act.wait_ge(scan_seq, 1)
            A(Hb[:, 0:NCC, :, :], HH[:, NCC - 1::-1, :, 1, :], ACT.Copy).then_inc(hb_ready, 1)
            A(Hb[:, NCC:NCH, :, :], HH[:, NCH - 1:NCC - 1:-1, :, 1, :], ACT.Copy).then_inc(hb_ready, 1)
            act.wait_ge(cb_ev, KS + 1)
            for m in range(KS):
                square(mix[:, KS + m, :], SQ_CONV + m, sq)
                roots(SQ_CONV + m + 1, rs, 6, 7, DC // 8, XS_CONV + m)
            for m in range(KS):
                act.wait_ge(y_ev, 2 * m + 2)
                ym = Y[:, :, m * P:(m + 1) * P]
                A(ym, ym, ACT.Gelu_apprx_tanh).then_inc(y_gelu, 1)
            for n in range(2 * KS):
                act.wait_ge(gt_mm, n + 1)
                cb_, th = n // 2, n % 2
                A(gT[:, cb_, :].rearrange("p (c t) -> p t c", t=Q)[:, 4 * th:4 * th + 4, :],
                  bank[2 + n % 2][:, 0:4 * NCH].rearrange("p (t c) -> p t c", t=4), ACT.Copy).then_inc(gt_ev, 1)
            for m in range(KS):
                act.wait_ge(z_mm, NCONV + m + 1)
                A(mix[:, m, CTX:T], bank[m % 2][:, :], ACT.Sigmoid, bias=col(COL_BGLU + m)).then_inc(glu_sig, 1)
                A(mix[:, m, 0:CTX], bank[2 + m % 2][:, 0:CTX], ACT.Sigmoid, bias=col(COL_BGLU + m)).then_inc(glu_sig, 1)
            act.wait_ge(y_mm, NG // 4)
            for m in range(KS):
                act.wait_ge(glu_ev, m + 1)
                square(mix[:, m, :], SQ_SSM + m, sq2)
            roots(SQ_SSM + KS, rs2, 4, 5, DS, 0)
            for k in range(KD):
                act.wait_ge(x1_ready, 2 * k + 2)
                square(xt[:, k, :], SQ_2 + k, sq2)
            roots(SQ_2 + KD, rs2, 4, 5, D, XS_SSM + 1)
            act.wait_ge(mod_ready, 2)
            act.wait_ge(xs_ready, XS_2 + 1)
            for k in range(KD):
                modulate(3, k, 0, 0, CTX).then_inc(h_ready, 1)

            def stage(t, blk):
                act.wait_ge(q_mm, t)
                A(h2Tc[:, :, :], hT[:, :, bass.ds(blk * P, P)], ACT.Copy).then_inc(h2_staged, 1)

            def take_q(t):
                act.wait_ge(q_mm, t + 1)
                A(q_s, bank[2][:, 0:DQ], ACT.Copy).then_inc(q_ev, 1)

            def take_qt(t):
                act.wait_ge(qt_mm, t + 1)
                A(qT.rearrange("p h t -> p (h t)"), bank[3][:, 0:DQ], ACT.Copy).then_inc(qt_ev, 1)

            def take_scores(t):
                act.wait_ge(sc_mm, t + 1)
                A(sc.rearrange("p h t -> p (h t)"), bank[6][:, 0:DQ], ACT.Copy).then_inc(sc_ev, 1)

            def exps(t):
                act.wait_ge(cand_ready, t + 1)
                A(e16, top, ACT.Exp, bias=small[:, 0:1], accum_out=small[:, 1:2]).then_inc(exp_done, 1)

            def gelu(G, par, k):
                act.wait_ge(dot_done, G * TOPK + (k + 1))
                A(gel[:, par, k:k + 1], hid[:, par, k:k + 1], ACT.Gelu_apprx_tanh).then_inc(gelu_done, 1)

            act.wait_ge(h_ready, 2 * KD)
            A(h2Tc[:, :, :], hT[:, :, 0:P], ACT.Copy).then_inc(h2_staged, 1)
            take_q(0)
            take_qt(0)
            take_scores(0)
            for k in range(KD):
                act.wait_ge(xs_ready, XS_2 + 1 + k + 1)
                modulate(3, k, 1, CTX, T).then_inc(h_ready, 1)
            exps(0)
            act.wait_ge(h_ready, 3 * KD)
            with nc.scalar.Fori(0, NBLK) as b:
                act.wait_ge(h2c_mm, b + 1)
                A(h2c[:, 0:512], bank[4][:, :], ACT.Copy)
                A(h2c[:, 512:1024], bank[5][:, :], ACT.Copy).then_inc(h2c_ready, 1)
                with nc.scalar.Fori(0, HEADS // 2) as hp:
                    for e in range(2):
                        G = b * HEADS + hp * 2 + e
                        t = G + 1
                        stage(t, (t // HEADS) % NBLK)
                        gelu(G, e, 0)
                        take_q(t)
                        gelu(G, e, 1)
                        take_qt(t)
                        gelu(G, e, 2)
                        take_scores(t)
                        for k in range(3, EXP_AT):
                            gelu(G, e, k)
                        exps(t)
                        for k in range(EXP_AT, TOPK):
                            gelu(G, e, k)
                act.wait_ge(v_done, b * (HEADS * TOPK) + (HEADS * TOPK + SLOTS))
                act.wait_ge(out_dma, b * 16 + 16)
                A(peer[:, 0:512], bank[0][:, :], ACT.Copy)
                A(peer[:, 512:1024], bank[1][:, :], ACT.Copy).then_inc(peer_ev, 1)
                act.wait_ge(x2_ready, b + 1)
                A(peer.rearrange("p (k t) -> p k t", k=KD), xt[:, :, bass.ds(b * P, P)], ACT.Square).then_inc(fsq_ready, 1)
                act.wait_ge(fs_mm, b + 1)
                A(frs[:, :], bank[7][:, 0:P], ACT.Sqrt, scale=1.0 / D, bias=eps_c[:, 0:1]).then_inc(frt, 1)

        @block.vector
        def _(dve):
            V = nc.vector
            link = Chain(dve, dve_seq)
            tt, ts, stt = V.tensor_tensor, V.tensor_scalar, V.scalar_tensor_tensor
            dve.wait_ge(ld_ssm, 32)
            dve.wait_ge(ssm_act, 1)
            lre, lim, dt = ssmv[:, 0, :], ssmv[:, 1, :], sv[:, 0, :]
            tt(sv[:, 1, :], lre, dt, ALU.mult).then_inc(ssm_dve, 1)
            link(tt(sv[:, 2, :], lim, dt, ALU.mult))
            link(ts(sv[:, 8, :], sv[:, 2, :], 1.0 / TWO_PI, None, ALU.mult))
            link(V.tensor_copy(kint[:, :], sv[:, 8, :]))
            link(V.tensor_copy(sv[:, 8, :], kint[:, :]))
            link(stt(sv[:, 4, :], sv[:, 8, :], -C1, sv[:, 2, :], ALU.mult, ALU.add))
            link(stt(sv[:, 4, :], sv[:, 8, :], -C2, sv[:, 4, :], ALU.mult, ALU.add))
            link(stt(sv[:, 4, :], sv[:, 8, :], -C3, sv[:, 4, :], ALU.mult, ALU.add))
            link(ts(sv[:, 5, :], sv[:, 4, :], TWO_PI / 4, None, ALU.add))
            link(ts(sv[:, 9, :], sv[:, 5, :], TWO_PI / 2, -TWO_PI, ALU.is_gt, ALU.mult))
            link(tt(sv[:, 5, :], sv[:, 5, :], sv[:, 9, :], ALU.add))
            link(ts(sv[:, 5, :], sv[:, 5, :], PI_IN, -PI_IN, ALU.min, ALU.max))
            ts(sv[:, 4, :], sv[:, 4, :], PI_IN, -PI_IN, ALU.min, ALU.max).then_inc(ssm_dve, 1)
            dve.wait_ge(ssm_act, 4)

            def cmul(o, a, b, t):
                link(tt(o[0], a[0], b[0], ALU.mult), tt(t, a[1], b[1], ALU.mult))
                link(tt(o[0], o[0], t, ALU.subtract))
                link(tt(o[1], a[0], b[1], ALU.mult), tt(t, a[1], b[0], ALU.mult))
                link(tt(o[1], o[1], t, ALU.add))

            link(V.memset(P9[:, 0, 0, :], 1.0), V.memset(P9[:, 0, 1, :], 0.0))
            link(tt(P9[:, 1, 0, :], sv[:, 3, :], sv[:, 7, :], ALU.mult),
                 tt(P9[:, 1, 1, :], sv[:, 3, :], sv[:, 6, :], ALU.mult))
            n = 1
            while n < Q:
                o = [P9[:, n + 1:2 * n + 1, r, :] for r in range(2)]
                x = [P9[:, n:n + 1, r, :].broadcast_to([P, n, NQ]) for r in range(2)]
                y = [P9[:, 1:n + 1, r, :] for r in range(2)]
                cmul(o, x, y, sv[:, 8:8 + n, :])
                n *= 2
            link(*[V.tensor_copy(P9r[:, j, :, :], P9[:, Q - j, :, :]) for j in range(Q + 1)])
            link(V.tensor_copy(AR[:, 0, :], P9[:, Q, 0, :]), V.tensor_copy(AR[:, 1, :], P9[:, Q, 0, :]),
                 V.tensor_copy(AI[:, 1, :], P9[:, Q, 1, :]), ts(AI[:, 0, :], P9[:, Q, 1, :], -1.0, None, ALU.mult))
            V.tensor_copy(sv[:, 11, :], sv[:, 3, :]).then_inc(p9_ready, 1)
            link(ts(sv[:, 0, :], P9[:, 1, 0, :], -1.0, None, ALU.add))
            link(tt(sv[:, 1, :], lre, lre, ALU.mult), tt(sv[:, 2, :], lim, lim, ALU.mult))
            link(tt(sv[:, 1, :], sv[:, 1, :], sv[:, 2, :], ALU.add))
            link(V.reciprocal(sv[:, 2, :], sv[:, 1, :]))
            im = P9[:, 1, 1, :]
            link(tt(sv[:, 4, :], sv[:, 0, :], lre, ALU.mult), tt(sv[:, 5, :], im, lim, ALU.mult))
            link(tt(sv[:, 4, :], sv[:, 4, :], sv[:, 5, :], ALU.add))
            link(tt(sv[:, 6, :], im, lre, ALU.mult), tt(sv[:, 7, :], sv[:, 0, :], lim, ALU.mult))
            link(tt(sv[:, 6, :], sv[:, 6, :], sv[:, 7, :], ALU.subtract))
            link(tt(sv[:, 4, :], sv[:, 4, :], sv[:, 2, :], ALU.mult), tt(sv[:, 6, :], sv[:, 6, :], sv[:, 2, :], ALU.mult))
            cf = [sv[:, v, :].rearrange("p (q a) -> p q a", a=1).broadcast_to([P, NQ, GC]) for v in (4, 6)]
            tb = tv.rearrange("p q s c -> p (q s c)")[:, 0:NQ * GC].rearrange("p (q c) -> p q c", q=NQ)
            cmul([Bb[:, 0, :, :], Bb[:, 1, :, :]], cf, [bcs[:, 0, :, :], bcs[:, 1, :, :]], tb)

            def chunk_inputs(d):
                w = P9r[:, 1:Q + 1] if d == 0 else P9[:, 0:Q]
                for h in range(2):
                    q = slice(d * NPAIR + 8 * h, d * NPAIR + 8 * h + 8)
                    pw = [w[:, :, r, q].rearrange("p s (q a) -> p q s a", a=1).broadcast_to([P, 8, Q, GC]) for r in range(2)]
                    bb = [Bb[:, r, q, :].rearrange("p q (a c) -> p q a c", a=1).broadcast_to([P, 8, Q, GC]) for r in range(2)]
                    cmul([BP[d][:, r, 8 * h:8 * h + 8, :, :] for r in range(2)], pw, bb, tv)
                V.tensor_copy(sv[:, 9, :], sv[:, 4, :]).then_inc(bp_ready, 1)

            chunk_inputs(0)
            chunk_inputs(1)

            def gains(sc_at, g_at, turn):
                dve.wait_ge(mod_free, turn)
                g = colv[:, g_at:g_at + KD].rearrange("p (k a) -> p k a", a=1).broadcast_to([P, KD, 2])
                stt(gs[:, :, :], modT[:, sc_at * KD:(sc_at + 1) * KD, :], 1.0, g, ALU.add, ALU.mult).then_inc(mod_ready, 1)

            def unroot(o, call, part=2):
                dve.wait_ge(rms_act, 2 * call + (1 if part == 0 else 2))
                o = (o[:, 0:CTX], o[:, CTX:T], o)[part]
                link(V.reciprocal(o, o))

            dve.wait_ge(ld_x, 16)
            unroot(rs, 0)
            for k in range(KD):
                tt(hT[:, k, :], hT[:, k, :], rs, ALU.mult).then_inc(xs_ready, 1)
            gains(1, COL_N1, NM1 + 2)
            dve.wait_ge(mod_mm, NM1)
            link(V.memset(Bd, 0.0))
            V.tensor_copy(Bd[0:64, :, :, 0:GC], Bb[0:64, :, :, :]).then_inc(bb_ready, 1)
            V.tensor_copy(Bd[64:128, :, :, GC:2 * GC], Bb[64:128, :, :, :]).then_inc(bb_ready, 1)
            dve.wait_ge(ld_dsk, 16)
            dve.wait_ge(ut_mm, NG // 4)
            tt(uc, uc, dsk.rearrange("p (g a c) -> p g a c", g=NG, a=1).broadcast_to([NCH, NG, Q, GC]), ALU.mult).then_inc(ud_ready, 1)
            for g in range(8):
                d, q4 = g // 4, slice((g % 4) * 4, (g % 4) * 4 + 4)
                dve.wait_ge(k_mm, g + 1)
                src = bank[2 + g % 2][0:2 * GC, :].rearrange("p (q x) -> p q x", q=4)
                dst = Ksb[:, q4, :]
                zero = (Q - 1) * GC
                if d == 0:
                    last = V.tensor_copy(dst[:, :, zero:], src)
                else:
                    link(V.tensor_copy(dst[:, :, 0:zero], src[:, :, 0:zero]))
                    last = tt(dst[:, :, zero:zero + GC], dst[:, :, zero:zero + GC], src[:, :, zero:], ALU.add)
                last.then_inc(k_ev, 1)
                dve.wait_ge(k_ev, g + 1)

            dve.wait_ge(k_out, 16)
            STEP = 12
            with nc.vector.Fori(0, KS) as i:
                cl = Chain(dve, conv_seq, i * STEP)
                w = [colv[:, bass.ds(i + (COL_CW + tap * KS), 1)] for tap in range(3)]
                dve.wait_ge(cc_ev, i + 2)
                dve.wait_ge(z_mm, i * 3 + 2)
                cl(tt(pr_t[:, CTX:T], cc_t[:, CTX:T], bank[1][:, :], ALU.mult))
                tt(pr_t[:, 0:CTX], cc_t[:, 0:CTX], bank[4][:, 0:CTX], ALU.mult).then_inc(ch_ev, 1)
                dve.wait_ge(ch_ev, i + 2)
                cl(ts(cv_t, pr_t, w[1], colv[:, bass.ds(i + COL_CB, 1)], ALU.mult, ALU.add))
                for lo, hi, rw in ((0, CTX, CTX), (CTX, T, ROW_W)):
                    pv = pr_t[:, lo:hi].rearrange("p (r w) -> p r w", w=rw)
                    cv = cv_t[:, lo:hi].rearrange("p (r w) -> p r w", w=rw)
                    cl(stt(cv[:, :, 1:rw], pv[:, :, 0:rw - 1], w[0], cv[:, :, 1:rw], ALU.mult, ALU.add))
                    cl(stt(cv[:, :, 0:rw - 1], pv[:, :, 1:rw], w[2], cv[:, :, 0:rw - 1], ALU.mult, ALU.add))
                dve.wait_ge(z_mm, i * 3 + 3)
                out = mix[:, bass.ds(i + KS, 1), :].rearrange("p a t -> p (a t)")
                cl(tt(out[:, CTX:T], cv_t[:, CTX:T], bank[2][:, :], ALU.mult))
                while cl.n < STEP:
                    cl(tt(small[:, 2:3], eps_c[:, :], eps_c[:, :], ALU.mult))
                tt(out[:, 0:CTX], cv_t[:, 0:CTX], bank[5][:, 0:CTX], ALU.mult).then_inc(cb_ev, 1)
                dve.wait_ge(cb_ev, i + 2)

            dve.wait_ge(ud_ready, 1)
            for g4 in range(NG // 4):
                dve.wait_ge(y_mm, g4 + 1)
                for j in range(4):
                    g = 2 * (4 * (g4 // 2) + j) + g4 % 2
                    cj = slice(g * GC, (g + 1) * GC)
                    last = tt(Y[:, :, cj], bank[g4 % 2][0:NCH, j * P:(j + 1) * P].rearrange("p (t c) -> p t c", t=Q),
                              uc[:, g, :, :], ALU.add)
                last.then_inc(y_ev, 1)
                if g4 in NORM_AT:
                    m = NORM_AT.index(g4)
                    unroot(rs, RT_CONV + m)
                    stt(mix[:, KS + m, :], mix[:, KS + m, :], col(COL_OG + KS + m), rs, ALU.mult, ALU.mult).then_inc(mix_ready, 1)
                    dve.wait_ge(mix_ready, m + 1)
                    V.tensor_copy(small[:, 2:3], eps_c[:, :]).then_inc(xs_ready, 1)
            dve.wait_ge(gt_ev, 2 * KS)
            for m in range(KS):
                dve.wait_ge(glu_sig, 2 * (m + 1))
                tt(mix[:, m, :], mix[:, m, :], gT[:, m, :], ALU.mult).then_inc(glu_ev, 1)
            unroot(rs2, RT_SSM)
            for m in range(KS):
                stt(mix[:, m, :], mix[:, m, :], col(COL_OG + m), rs2, ALU.mult, ALU.mult).then_inc(mix_ready, 1)
            dve.wait_ge(mix_ready, KD)
            V.tensor_copy(small[:, 2:3], eps_c[:, :]).then_inc(xs_ready, 1)
            gains(4, COL_N2, NMT // MCH + 2)
            dve.wait_ge(ld_x2, 16)
            for m in range(KD):
                dve.wait_ge(z_mm, NCONV + KS + m + 1)
                g1 = modT[:, 2 * KD + m, :]
                stt(xt[:, m, CTX:T], bank[m % 2][:, :], g1[:, 1:2], xt[:, m, CTX:T], ALU.mult, ALU.add).then_inc(x1_ready, 1)
                stt(xt[:, m, 0:CTX], bank[2 + m % 2][:, 0:CTX], g1[:, 0:1], xt[:, m, 0:CTX], ALU.mult, ALU.add).then_inc(x1_ready, 1)
            dve.wait_ge(x1_ready, 2 * KD)
            unroot(rs2, RT_2, 0)
            tt(hT[:, :, 0:CTX], xt[:, :, 0:CTX], rs2[:, 0:CTX].rearrange("p (a t) -> p a t", a=1).broadcast_to([P, KD, CTX]),
               ALU.mult).then_inc(xs_ready, 1)
            unroot(rs2, RT_2, 1)
            for k in range(KD):
                tt(hT[:, k, CTX:T], xt[:, k, CTX:T], rs2[:, CTX:T], ALU.mult).then_inc(xs_ready, 1)
            for b in range(NBLK):
                last = V.tensor_copy(g2b[:, b, :], modT[:, 5 * KD:6 * KD, min(b, 1)])
            link(last)

            NT = 26

            def best_keys(cl, t):
                dve.wait_ge(sc_ev, t + 1)
                dve.nop(nofuse=True)
                cl(*[V.max(m16[:, h, 0:8], sc[:, h, :]) for h in range(2)], hold=True)
                cl(*[V.max_index(i16[:, h, 0:8], m16[:, h, 0:8], sc[:, h, :]) for h in range(2)],
                   *[V.match_replace(sc2[:, h, :], m16[:, h, 0:8], sc[:, h, :], NEG) for h in range(2)], hold=True)

            def next_keys(cl, t):
                cl(*[V.max(m16[:, h, 8:16], sc2[:, h, :]) for h in range(2)], hold=True)
                cl(*[V.max_index(i16[:, h, 8:16], m16[:, h, 8:16], sc2[:, h, :]) for h in range(2)])

            def best_sums(cl, t):
                c2 = cand.rearrange("p (a b) -> p a b", a=TOPK)
                cl(tt(c2, m16[:, 0, :].rearrange("p (a b) -> p a b", b=1).broadcast_to([P, TOPK, TOPK]),
                      m16[:, 1, :].rearrange("p (a b) -> p a b", a=1).broadcast_to([P, TOPK, TOPK]), ALU.add), hold=True)
                cl(V.max(top[:, 0:8], cand), hold=True)
                cl(V.max_index(pos[:, 0:8], top[:, 0:8], cand), V.match_replace(cand2, top[:, 0:8], cand, NEG), hold=True)

            def next_sums(cl, t):
                cl(V.max(top[:, 8:16], cand2), ts(small[:, 0:1], top[:, 0:1], -1.0, None, ALU.mult), hold=True)
                V.max_index(pos[:, 8:16], top[:, 8:16], cand2).then_inc(cand_ready, 1)
                dve.wait_ge(cand_ready, t + 1)

            def match_places(cl, t):
                cl(ts(ab[:, :, 0], pos[:, :], 4, None, ALU.logical_shift_right), ts(ab[:, :, 1], pos[:, :], 15, None, ALU.bitwise_and),
                   ts(i12[:, 0, :], i16[:, 0, :], float(NKEY), None, ALU.mult), V.tensor_copy(i12[:, 1, :], i16[:, 1, :]))
                cl(tt(e4, ab[:, :, :].rearrange("p k (h j) -> p k h j", j=1).broadcast_to([P, TOPK, 2, TOPK]),
                      iota[:, :].rearrange("p (k h j) -> p k h j", k=1, h=1).broadcast_to([P, TOPK, 2, TOPK]), ALU.is_equal))

            def experts_and_gates(cl, t, par):
                cl(tt(e4, e4, i12.rearrange("p (k h) j -> p k h j", k=1).broadcast_to([P, TOPK, 2, TOPK]), ALU.mult))
                cl(V.tensor_reduce(idf, eq.rearrange("p (k x) -> p k x", k=TOPK), AX.X, ALU.add))
                cl(V.tensor_copy(gidx[:, par, :], idf))
                dve.wait_ge(exp_done, t + 1)
                cl(V.reciprocal(small[:, 3:4], small[:, 1:2]))
                cl(ts(gate[:, par, :], e16, small[:, 3:4], None, ALU.mult))
                V.tensor_copy(small[:, 2:3], small[:, 3:4]).then_inc(topk_done, 1)

            def topk_stage(cl, t, par, n):
                if n < 5:
                    (best_keys, next_keys, best_sums, next_sums, match_places)[n](cl, t)
                else:
                    experts_and_gates(cl, t, par)

            e4 = eq.rearrange("p (k h j) -> p k h j", k=TOPK, h=2)

            def dot(G, par, k):
                s = k % SLOTS
                dve.wait_ge(row_in[s], G * 32 + (k // SLOTS + 1) * 16)
                V.tensor_tensor_reduce(rows[:, s, 0:D], rows[:, s, 0:D], h2c, 1.0, 0.0, ALU.mult, ALU.add,
                                       hid[:, par, k:k + 1]).then_inc(dot_done, 1)

            def make_diag(G, par, k):
                dve.wait_ge(gelu_done, G * TOPK + (k + 1))
                dve.wait_ge(v_done, G * TOPK + (k + SLOTS - 3))
                ts(diag[:, k % 4, :], ident[:, :], gel[:, par, k:k + 1], gate[:, par, k:k + 1], ALU.mult, ALU.mult).then_inc(diag_ready, 1)

            cl = Chain(dve, topk_seq)
            for n in range(6):
                topk_stage(cl, 0, 0, n)
            assert cl.n == NT, cl.n
            with nc.vector.Fori(0, NBLK) as b:
                dve.wait_ge(h2c_ready, b + 1)
                dve.nop(nofuse=True)
                with nc.vector.Fori(0, HEADS // 2) as hp:
                    for e in range(2):
                        G = b * HEADS + hp * 2 + e
                        t = G + 1
                        cl = Chain(dve, topk_seq, t * NT)
                        for k in range(TOPK):
                            if TOPK_AT <= k < TOPK_AT + 6:
                                topk_stage(cl, t, 1 - e, k - TOPK_AT)
                            dot(G, e, k)
                            if k:
                                make_diag(G, e, k - 1)
                        make_diag(G, e, TOPK - 1)
                fl = Chain(dve, fin_seq, b * 6)
                pk = peer.rearrange("p (k t) -> p k t", k=KD)
                xb = xt[:, :, bass.ds(b * P, P)]
                dve.wait_ge(pt_mm, b + 1)
                for h in range(2):
                    g2 = g2b[:, bass.ds(b, 1), 4 * h:4 * h + 4].rearrange("p a (k c) -> p (a k) c", c=1).broadcast_to([P, 4, P])
                    last = tt(pk[:, 4 * h:4 * h + 4, :], bank[4 + h][:, :].rearrange("p (k t) -> p k t", k=4), g2, ALU.mult)
                    fl(last)
                tt(xb, xb, pk, ALU.add).then_inc(x2_ready, 1)
                dve.wait_ge(frt, b + 1)
                fl(V.reciprocal(frs[:, :], frs[:, :]))
                fl(tt(pk, xb, frs[:, :].rearrange("p (a t) -> p a t", a=1).broadcast_to([P, KD, P]), ALU.mult))
                while fl.n < 6:
                    fl(V.tensor_copy(small[:, 2:3], eps_c[:, :]))
                nf = colv[:, COL_NF:COL_NF + KD].rearrange("p (k a) -> p k a", a=1).broadcast_to([P, KD, P])
                tt(pk, pk, nf, ALU.mult).then_inc(out_ready, 1)

        @block.gpsimd
        def _(pool):
            G_ = nc.gpsimd
            link = Chain(pool, pool_seq)
            link(G_.memset(ident[:, :], 0.0), G_.memset(ones[:, :], 1.0), G_.memset(zeros[:, :], 0.0),
                 G_.memset(headones[:, :], 0.0), G_.memset(eps_c[:, :], EPS))
            link(G_.affine_select(out=ident[:, :], in_=ident[:, :], compare_op=ALU.not_equal, fill=1.0, base=0,
                                  pattern=[[-1, P]], channel_multiplier=1))
            link(G_.memset(headones[0:64, 0:64], 1.0), G_.memset(headones[64:128, 64:128], 1.0))
            G_.iota(iota[:, :], [[1, TOPK]], base=0, channel_multiplier=0, allow_small_or_imprecise_dtypes=True).then_inc(consts, 1)
            pool.wait_ge(p9_ready, 1)
            pool.wait_ge(ld_ssm, 32)
            for q4 in range(0, NQ, 4):
                q = slice(q4, q4 + 4)
                w = P9 if q4 < NPAIR else P9r
                J = Q + 1
                pw = [w[:, :, r, q].rearrange("p s (q a) -> p q s a", a=1).broadcast_to([P, 4, J, GC]) for r in range(2)]
                cv = [bcs[:, 2 + r, q, :].rearrange("p q (a c) -> p q a c", a=1).broadcast_to([P, 4, J, GC]) for r in range(2)]
                o = [CP[:, r, q, :, :] for r in range(2)]
                T_ = G_.tensor_tensor
                link(T_(o[0], pw[0], cv[0], ALU.mult), T_(tp, pw[1], cv[1], ALU.mult))
                link(T_(o[0], o[0], tp, ALU.subtract))
                link(T_(o[1], pw[0], cv[1], ALU.mult), T_(tp, pw[1], cv[0], ALU.mult))
                link(T_(o[1], o[1], tp, ALU.add))
                link(G_.tensor_scalar(o[1], o[1], -1.0, None, ALU.mult))
            G_.memset(scan_a[:, :, :], 0.0).then_inc(cp_ready, 1)
            pool.wait_ge(s_ev, 16)
            pool.wait_ge(cp_ready, 1)
            link(G_.tensor_copy(fin[:, :, :], HHs[:, NCC, :, :]))
            link(G_.tensor_copy(HHs[:, NCC, :, :], ssmv[:, 3:5, :]), G_.memset(HHs[:, 0, :, :], 0.0))

            def step(cl, prev, cur, hold):
                cl(G_.tensor_tensor(scan_a[:, :, :], prev, AR[:, :, :], ALU.mult),
                   G_.tensor_tensor(scan_b[:, 0, :], prev[:, 1, :], AI[:, 0, :], ALU.mult),
                   G_.tensor_tensor(scan_b[:, 1, :], prev[:, 0, :], AI[:, 1, :], ALU.mult), hold=hold)
                cl(G_.tensor_tensor(scan_a[:, :, :], scan_a[:, :, :], cur, ALU.add), hold=hold)
                cl(G_.tensor_tensor(cur, scan_a[:, :, :], scan_b[:, :, :], ALU.add), hold=hold)

            def at(slot):
                return HHs[:, bass.ds(slot, 1), :, :].rearrange("p a r x -> p (a r) x")

            base, STEP_OPS = link.n, 5
            for first, steps in ((0, NCC - 1), (NCC, NCL - 1)):
                with nc.gpsimd.Fori(0, steps // 3) as i:
                    cl = Chain(pool, pool_seq, i * (3 * STEP_OPS) + base)
                    for j in range(3):
                        step(cl, at(i * 3 + (first + j)), at(i * 3 + (first + j + 1)), True)
                base += steps * STEP_OPS
            link.n = base
            step(link, HHs[:, NCC - 1, :, :], fin[:, :, :], False)
            G_.memset(scan_a[:, :, :], 0.0).then_inc(scan_seq, 1)
            pool.sem_inc(v_done, SLOTS)
            with nc.gpsimd.Fori(0, NBLK * HEADS // 2) as g2:
                for e in range(2):
                    G = g2 * 2 + e
                    pool.wait_ge(topk_done, G + 1)
                    for k in range(TOPK):
                        pool.wait_ge(v_done, G * TOPK + (k + 1))
                        pool.nop(nofuse=True)
                        G_.indirect_dma_start(rows[:, k % SLOTS, :], None, table,
                                              bass.IndirectOffsetOnAxis(gidx[:, e, k:k + 1], 0)).then_inc(row_in[k % SLOTS], 16)
    return nc


def _layout(i):
    import numpy as np

    def colt(v):
        return np.asarray(v).reshape(-1, P).T

    a = {k: np.asarray(v) for k, v in i.items()}
    x = np.concatenate([a["x_prompt"][0], a["x_sample"][0]], axis=0)
    out = {"xT": x.reshape(T, KD, P).transpose(2, 1, 0)}
    out["condT"] = np.stack([a["c_ctx"], a["c"][0]]).reshape(2, KD, P).transpose(2, 1, 0)
    out["cols"] = np.concatenate(
        [colt(a["b_mod"][0]), colt(a["norm1_g"][0]), colt(a["norm2_g"][0]), colt(a["final_norm_g"]),
         colt(a["b_glu"][0]), colt(a["conv_w"][0]), colt(a["conv_b"][0]), colt(a["out_norm_g"][0])], axis=1)
    out["w_mod"] = a["w_mod"][0]
    w_in = a["w_in"][0]
    out["w_u"] = w_in[:, :DS].reshape(KD, P, DS).transpose(1, 0, 2)

    def tiles(w):
        return w.reshape(w.shape[0] // P, P, -1, P).transpose(2, 1, 0, 3)

    cb, cc, ch = (tiles(w_in[:, DS + j * DC:DS + (j + 1) * DC]) for j in range(3))
    conv = np.stack([cc, ch, cb], axis=1).reshape(3 * KS, P, KD, P)
    glu = tiles(a["w_glu"][0]).reshape(KS // 2, 2, P, KS, P).transpose(0, 2, 1, 3, 4)
    out["w_tiles"] = np.concatenate([conv, glu.reshape(KS // 2, P, KD, P)], axis=0)
    out["w_o"] = tiles(a["w_out"][0]).transpose(1, 0, 2, 3)

    def states(v):
        v = v.reshape((2, NPAIR, 2, NS) + v.shape[3:])
        v = np.moveaxis(v, (2, 3), (0, 1))
        return v.reshape((P, NQ) + v.shape[4:])

    dt = np.broadcast_to(a["log_dt"][0][:, :, None], (2, NG, NS))
    out["ssm"] = np.stack([states(v) for v in (a["lam_re"][0], a["lam_im"][0], dt, a["state_ssm_re"][0, 0], a["state_ssm_im"][0, 0])], axis=1)
    out["bc"] = np.stack([states(a["b_re"][0]), states(a["b_im"][0]),
                          states(a["c_re"][0].transpose(0, 1, 3, 2)), states(a["c_im"][0].transpose(0, 1, 3, 2))], axis=1)
    out["dskip"] = np.broadcast_to(a["d_skip"][0][None], (NCH, DS))
    out["skT"] = a["sub_keys"][0].transpose(2, 0, 1)
    out["w_query"] = a["w_query"][0].reshape(KD, P, -1).transpose(1, 0, 2)
    out["table"] = np.concatenate([a["expert_u"][0], a["expert_v"][0]], axis=1)
    return {k: np.ascontiguousarray(v) for k, v in out.items()}


def kernel(**inputs):
    import numpy as np
    import concourse.bacc as bacc
    from concourse.bass_utils import run_bass_kernel_spmd

    arrays = _layout(inputs)
    nc = bacc.Bacc("TRN2", target_bir_lowering=False, num_devices=1)
    args = [nc.dram_tensor(n, a.shape, mybir.dt.from_np(a.dtype), kind="ExternalInput").ap() for n, a in arrays.items()]
    args.append(nc.dram_tensor("y_out", (P, KD, T), F32, kind="ExternalOutput").ap())
    args.append(nc.dram_tensor("st_out", (P, 2, NQ), F32, kind="ExternalOutput").ap())
    args.append(nc.dram_tensor("kfull", (DS, NLAG * GC), F32, kind="Internal").ap())
    build(nc, *args)
    r = run_bass_kernel_spmd(nc, [arrays], core_ids=[0]).results[0]
    y = np.ascontiguousarray(r["y_out"].transpose(2, 1, 0)).reshape(T, D)
    st = r["st_out"].reshape(2, NS, 2, 2, NPAIR).transpose(2, 3, 4, 0, 1).reshape(2, 1, 1, 2, NG, NS)
    return (np.ascontiguousarray(y[:CTX]).reshape(1, CTX, D), np.ascontiguousarray(y[CTX:]).reshape(1, LAT, D),
            np.ascontiguousarray(st[0]), np.ascontiguousarray(st[1]))
```
